# Optimizing a Trainium2 kernel written in Bass

```python
import jax, jax.numpy as jnp
from jax import lax
import numpy as np

D_MODEL = 1024
BATCH = 1
SEQ = 256
DEPTH = 2

D_PLE = 256
HEAD_DIM = 64
FOX_WIDTH = D_MODEL // 2
FOX_HEADS = FOX_WIDTH // HEAD_DIM
HGRN_WIDTH = D_MODEL // 2
HGRN_HEADS = HGRN_WIDTH // HEAD_DIM
HGRN_KEY_DIM = HEAD_DIM
HGRN_VAL_DIM = HEAD_DIM
D_MIX = FOX_WIDTH + HGRN_WIDTH
IN_SPLIT_SIZES = (FOX_WIDTH, FOX_WIDTH, FOX_WIDTH, FOX_HEADS, HGRN_WIDTH, HGRN_WIDTH, HGRN_WIDTH, HGRN_WIDTH)
D_IN = sum(IN_SPLIT_SIZES)
IN_SPLIT_IDX = tuple(int(v) for v in np.cumsum(IN_SPLIT_SIZES)[:-1])
Q_BLOCK = 128
CHUNK = 64
D_FF = 2816
N_EXPERTS = 8
TOP_K = 2
D_EXPERT = 3584
N_DENSE = (DEPTH + 1) // 2
N_MOE = DEPTH // 2
EPS = 1e-6

kernel_name = "hybrid_fox_hgrn2_moe_ple_trunk"

def rmsnorm(x, gain):
    xf = x.astype(jnp.float32)
    y = xf * lax.rsqrt(jnp.mean(xf * xf, axis=-1, keepdims=True) + EPS)
    return (y * gain.astype(jnp.float32)).astype(x.dtype)

def head_rmsnorm(x, gain, n_heads):
    b, s, w = x.shape
    xh = x.reshape(b, s, n_heads, w // n_heads)
    return rmsnorm(xh, gain.reshape(n_heads, w // n_heads)).reshape(b, s, w)

def forgetting_attention(q, k, v, fgate_logit, fgate_bias):
    b, s, _ = q.shape
    h, dh = FOX_HEADS, HEAD_DIM
    q = q.reshape(b, s, h, dh)
    k = k.reshape(b, s, h, dh)
    v = v.reshape(b, s, h, dh)
    log_f = jax.nn.log_sigmoid(fgate_logit.astype(jnp.float32) + fgate_bias.astype(jnp.float32))
    c = jnp.cumsum(log_f, axis=1).transpose(0, 2, 1)
    nb = s // Q_BLOCK
    q_blocks = q.reshape(b, nb, Q_BLOCK, h, dh).transpose(1, 0, 3, 2, 4)
    c_blocks = c.reshape(b, h, nb, Q_BLOCK).transpose(2, 0, 1, 3)
    starts = jnp.arange(nb, dtype=jnp.int32) * Q_BLOCK
    k_pos = jnp.arange(s, dtype=jnp.int32)
    scale = dh ** -0.5

    def attend_block(args):
        q_blk, c_blk, start = args
        logits = jnp.einsum('bhqd,bkhd->bhqk', q_blk, k, preferred_element_type=jnp.float32) * scale
        logits = logits + c_blk[..., None] - c[:, :, None, :]
        q_pos = start + jnp.arange(Q_BLOCK, dtype=jnp.int32)
        causal = k_pos[None, :] <= q_pos[:, None]
        probs = jax.nn.softmax(jnp.where(causal, logits, -jnp.inf), axis=-1)
        return jnp.einsum('bhqk,bkhd->bqhd', probs.astype(v.dtype), v)

    out = lax.map(attend_block, (q_blocks, c_blocks, starts))
    return out.transpose(1, 0, 2, 3, 4).reshape(b, s, h * dh)

def hgrn2_recurrence(q, f_logit, i_in, lower_bound):
    b, s, _ = q.shape
    h, dk, dv = HGRN_HEADS, HGRN_KEY_DIM, HGRN_VAL_DIM
    f32 = jnp.float32
    lb = lower_bound.astype(f32).reshape(h, dk)
    log_f = jnp.logaddexp(jnp.log(lb), jnp.log1p(-lb) + jax.nn.log_sigmoid(f_logit.astype(f32).reshape(b, s, h, dk)))
    key = -jnp.expm1(log_f)
    nc = s // CHUNK

    def to_chunks(a, d):
        return a.reshape(b, nc, CHUNK, h, d).transpose(1, 0, 3, 2, 4)

    q_c = to_chunks(q.astype(f32), dk)
    k_c = to_chunks(key, dk)
    v_c = to_chunks(i_in.astype(f32), dv)
    b_c = jnp.cumsum(to_chunks(log_f, dk), axis=3)
    causal = jnp.tril(jnp.ones((CHUNK, CHUNK), dtype=bool))[:, :, None]

    def chunk_step(state, inp):
        q_t, k_t, v_t, b_t = inp
        decay = jnp.exp(jnp.where(causal, b_t[:, :, :, None, :] - b_t[:, :, None, :, :], -jnp.inf))
        scores = jnp.einsum('bhtd,bhsd,bhtsd->bhts', q_t, k_t, decay)
        out = jnp.einsum('bhts,bhsv->bhtv', scores, v_t) + jnp.einsum('bhtd,bhdv->bhtv', q_t * jnp.exp(b_t), state)
        b_end = b_t[:, :, -1:, :]
        new_state = jnp.exp(b_end[:, :, 0, :])[..., None] * state + jnp.einsum('bhsd,bhsv->bhdv', k_t * jnp.exp(b_end - b_t), v_t)
        return new_state, out

    state0 = jnp.zeros((b, h, dk, dv), f32)
    _, o = lax.scan(chunk_step, state0, (q_c, k_c, v_c, b_c))
    return o.transpose(1, 0, 3, 2, 4).reshape(b, s, h * dv).astype(q.dtype)

def swiglu(u, w_gate, w_up, w_down):
    return (jax.nn.silu(u @ w_gate) * (u @ w_up)) @ w_down

def moe_swiglu(u, w_router, w_gate, w_up, w_down):
    b, s, d = u.shape
    t = u.reshape(b * s, d)
    logits = jnp.dot(t, w_router, preferred_element_type=jnp.float32)
    top_logit, top_idx = lax.top_k(logits, TOP_K)
    top_w = jax.nn.softmax(top_logit, axis=-1)
    gate = jnp.einsum('tk,tke->te', top_w, jax.nn.one_hot(top_idx, N_EXPERTS, dtype=jnp.float32)).astype(u.dtype)
    out = jnp.zeros_like(t)
    for e in range(N_EXPERTS):
        out = out + gate[:, e:e + 1] * swiglu(t, w_gate[e], w_up[e], w_down[e])
    return out.reshape(b, s, d)

def setup_inputs(seed: int = 0) -> dict:
    key = jax.random.key(seed)
    ks = jax.random.split(key, 21)

    def nrm(k, shape, scale):
        return jax.random.normal(k, shape, jnp.float32) * scale

    def gain(k, shape):
        return 1.0 + nrm(k, shape, 0.02)

    return {
        'x': nrm(ks[0], (BATCH, SEQ, D_MODEL), 1.0),
        'p': nrm(ks[1], (DEPTH, BATCH, SEQ, D_PLE), 1.0),
        'w_in': nrm(ks[2], (DEPTH, D_MODEL, D_IN), D_MODEL ** -0.5),
        'fox_gate_bias': 2.0 + nrm(ks[3], (DEPTH, FOX_HEADS), 0.5),
        'fox_out_gain': gain(ks[4], (DEPTH, FOX_WIDTH)),
        'hgrn_lb_logits': nrm(ks[5], (DEPTH, HGRN_WIDTH), 0.1),
        'hgrn_out_gain': gain(ks[6], (DEPTH, HGRN_WIDTH)),
        'w_out': nrm(ks[7], (DEPTH, D_MIX, D_MODEL), D_MIX ** -0.5),
        'mix_norm_gain': gain(ks[8], (DEPTH, D_MODEL)),
        'ffn_norm_gain': gain(ks[9], (DEPTH, D_MODEL)),
        'ple_norm_gain': gain(ks[10], (DEPTH, D_MODEL)),
        'w_ffn_gate': nrm(ks[11], (N_DENSE, D_MODEL, D_FF), D_MODEL ** -0.5),
        'w_ffn_up': nrm(ks[12], (N_DENSE, D_MODEL, D_FF), D_MODEL ** -0.5),
        'w_ffn_down': nrm(ks[13], (N_DENSE, D_FF, D_MODEL), D_FF ** -0.5),
        'w_router': nrm(ks[14], (N_MOE, D_MODEL, N_EXPERTS), D_MODEL ** -0.5),
        'w_exp_gate': nrm(ks[15], (N_MOE, N_EXPERTS, D_MODEL, D_EXPERT), D_MODEL ** -0.5),
        'w_exp_up': nrm(ks[16], (N_MOE, N_EXPERTS, D_MODEL, D_EXPERT), D_MODEL ** -0.5),
        'w_exp_down': nrm(ks[17], (N_MOE, N_EXPERTS, D_EXPERT, D_MODEL), D_EXPERT ** -0.5),
        'w_ple': nrm(ks[18], (DEPTH, D_PLE, D_MODEL), D_PLE ** -0.5),
        'w_ple_gate': nrm(ks[19], (DEPTH, D_MODEL, D_MODEL), D_MODEL ** -0.5),
        'final_norm_gain': gain(ks[20], (D_MODEL,)),
    }

def reference(x, p, w_in, fox_gate_bias, fox_out_gain, hgrn_lb_logits, hgrn_out_gain, w_out, mix_norm_gain, ffn_norm_gain, ple_norm_gain, w_ffn_gate, w_ffn_up, w_ffn_down, w_router, w_exp_gate, w_exp_up, w_exp_down, w_ple, w_ple_gate, final_norm_gain):
    lb_cum = jnp.cumsum(jax.nn.softmax(hgrn_lb_logits.astype(jnp.float32), axis=0), axis=0)
    lower_bounds = lb_cum - lb_cum[0:1]
    h = x
    for i in range(DEPTH):
        u = rmsnorm(h, mix_norm_gain[i])
        z = u @ w_in[i]
        fq, fk, fv, fg, hq, hf, hi, hg = jnp.split(z, IN_SPLIT_IDX, axis=-1)
        a_out = head_rmsnorm(forgetting_attention(fq, fk, fv, fg, fox_gate_bias[i]), fox_out_gain[i], FOX_HEADS)
        r_out = head_rmsnorm(hgrn2_recurrence(hq, hf, hi, lower_bounds[i]), hgrn_out_gain[i], HGRN_HEADS) * jax.nn.silu(hg)
        h = h + jnp.concatenate([a_out, r_out], axis=-1) @ w_out[i]
        u = rmsnorm(h, ffn_norm_gain[i])
        j = i // 2
        if i % 2 == 0:
            h = h + swiglu(u, w_ffn_gate[j], w_ffn_up[j], w_ffn_down[j])
        else:
            h = h + moe_swiglu(u, w_router[j], w_exp_gate[j], w_exp_up[j], w_exp_down[j])
        u = rmsnorm(h, ple_norm_gain[i])
        h = h + (p[i] @ w_ple[i]) * jax.nn.sigmoid(u @ w_ple_gate[i])
    return rmsnorm(h, final_norm_gain)


_drawn_inputs = setup_inputs


def setup_inputs(seed=0):
    import zlib

    import numpy as np

    out = dict(_drawn_inputs(seed))
    spreads = {}
    factors = {'hgrn_out_gain': 4.846,
     'ple_norm_gain': 40.115,
     'final_norm_gain': 25.621,
     'ffn_norm_gain': 2.877,
     'fox_out_gain': 2.723}
    for name, (base, spread) in spreads.items():
        noise = np.random.default_rng([zlib.crc32(name.encode()), seed]).standard_normal(out[name].shape)
        drawn = base * np.exp(spread * noise) if base else spread * noise
        out[name] = __import__('jax').numpy.asarray(drawn.astype(out[name].dtype))
    for name, factor in factors.items():
        out[name] = (out[name] * factor).astype(out[name].dtype)
    return out
```

```python
from contextlib import ExitStack

import concourse.bass as bass
from concourse import mybir

P = 128
DEPTH = 2
SEQ = 256
TT = SEQ // P
D = 1024
KT = D // P
DPLE = 256
PKT = DPLE // P
HD = 64
NH = 8
W = NH * HD
NP = NH // 2
DIN = 7 * W + NH
DFF = 2816
NE = 8
DEX = 3584
NC = 512
SLOT = KT * NC
RING_SLOTS = 7
FFR = (DFF + NC - 1) // NC
EXR = DEX // NC
OVER = (2 * SEQ) // (P + 1)
ITEMS = NE + OVER
EPS = 1e-6
NEG = -1.0e30
GATE_FLOOR = -80.0
LEVELS = [1, 2, 4, 8, 16, 32, 64]
NL = len(LEVELS) + 1

ALU = mybir.AluOpType
ACT = mybir.ActivationFunctionType
F32 = mybir.dt.float32
I32 = mybir.dt.int32
U32 = mybir.dt.uint32
AX = mybir.AxisListType.X

COL = dict(fq=0, fk=W, fv=2 * W, fg=3 * W, hq=3 * W + NH, hf=4 * W + NH, hi=5 * W + NH, hg=6 * W + NH)
IN_ORDER = ["hf", "hq", "fq", "fk", "fv", "hi", "hg"]

ROW_NORM = lambda k: (k % 3) * DEPTH * KT + (k // 3) * KT
ROW_OUT = 3 * DEPTH * KT
ROW_LB = ROW_OUT + DEPTH * KT
ROWS = ROW_LB + DEPTH * NP

EXP_ORDER = [("g", 0), ("u", 0)]
for _r in range(1, EXR):
    EXP_ORDER += [("g", _r), ("u", _r), ("d", _r - 1)]
EXP_ORDER += [("d", EXR - 1)]
EXP_LOADS = len(EXP_ORDER)
assert EXP_LOADS % RING_SLOTS == 0


def static_loads():
    order = []
    for l in range(DEPTH):
        order += [("in", l, c) for c in IN_ORDER] + [("out", l, n) for n in range(2)]
        if l == 0:
            for r in range(FFR):
                order += [("fg", l, r), ("fu", l, r), ("fd", l, r)]
            order += [("pe", l, 0)] + [("pg", l, n) for n in range(2)]
    return order


STATIC = static_loads()
NSTATIC = len(STATIC)
TAIL = [("pe", 1, 0), ("pg", 1, 0), ("pg", 1, 1)]


def trunk(nc, x, p, w_in, fox_gate_bias, fox_out_gain, hgrn_lb_logits, hgrn_out_gain, w_out,
          mix_norm_gain, ffn_norm_gain, ple_norm_gain, w_ffn_gate, w_ffn_up, w_ffn_down, w_router,
          w_exp_gate, w_exp_up, w_exp_down, w_ple, w_ple_gate, final_norm_gain, out):
    ctx = ExitStack()
    with ctx:
        def sb(name, shape, dt=F32):
            return ctx.enter_context(nc.sbuf_tensor(name, shape, dt))

        def sem(name):
            return ctx.enter_context(nc.semaphore(name))

        def sems(name, n):
            return [sem(f"{name}{i}") for i in range(n)]

        ring = sb("ring", [P, RING_SLOTS, SLOT])
        h = sb("h", [P, TT, D])
        un = sb("un", [P, TT, D])
        uT = sb("uT", [P, KT, SEQ])
        work = sb("work", [P, 12 * 1024])
        scores = sb("scores", [P, TT, NH, P])
        vec = sb("vec", [P, P])
        rows = sb("rows", [P, P])
        ident = sb("ident", [P, P])
        masks = sb("masks", [P, NL, P])
        causal = sb("causal", [P, P])
        before = sb("before", [P, P])
        ones = sb("ones", [P, SEQ])
        pick = sb("pick", [P, NH, P])
        wfg = sb("wfg", [P, KT, P])
        bias = sb("bias", [P, DEPTH])
        wr = sb("wr", [P, KT, NE])
        iota = sb("iota", [P, P])
        lb = sb("lb", [P, DEPTH, NP])
        oml = sb("oml", [P, DEPTH, NP])
        small = sb("small", [P, 512])
        item_expert = sb("item_expert", [P, ITEMS + 1], I32)
        negc = sb("negc", [P, SEQ])
        fgt = sb("fgt", [P, 2, SEQ])
        small_fg = [fgt[:, i, :] for i in range(2)]

        def region(at, *shape):
            n = 1
            for s in shape:
                n *= s
            v = work[:, at:at + n]
            if len(shape) == 2:
                return v.rearrange("p (a b) -> p a b", a=shape[0])
            if len(shape) == 3:
                return v.rearrange("p (a b c) -> p a b c", a=shape[0], b=shape[1])
            return v

        qT = region(0, NP, SEQ)
        kT = region(1024, NP, SEQ)
        fv = region(2048, TT, W)
        hqT = region(3072, NP, SEQ)
        hv = region(4096, TT, W)
        hgate = region(5120, TT, W)
        en = region(6144, NP, SEQ)
        cross = region(6144, NH, P)
        keyT = region(7168, NP, SEQ)
        bT = region(8192, NP, SEQ)
        arg = region(9216, NP, SEQ)
        xl = [region(10240 + 1024 * i, NP, SEQ) for i in range(2)]
        probs = [region(10240 + 512 * i, NC) for i in range(2)]
        probsT = [region(11264 + 512 * i, 4, P) for i in range(2)]
        sq = region(9216, TT, W)
        sqrow = [region(9216 + D * t, D) for t in range(TT)]
        ffs = [region(512 * i, SEQ) for i in range(2)]
        ffh = [region(1024 + 1024 * i, 4, SEQ) for i in range(2)]
        pn = region(8192, TT, DPLE)
        pT = region(8704, PKT, SEQ)
        sig = region(4096, TT, D)
        prod = region(6144, TT, D)
        uTe = region(0, KT, P)
        exs = [region(1024 + 512 * i, NC) for i in range(2)]
        exh = [region(2048 + 512 * i, NC) for i in range(2)]
        exhT = [region(3072 + 512 * i, 4, P) for i in range(2)]
        ye = region(4096, D)
        sel = region(5120, TT, P)
        selg = region(5376, TT, P)
        combT = region(5632, TT, P)
        fgain = region(0, D)
        fout = region(1024, TT, D)

        psum = [ctx.enter_context(nc.psum_tensor(f"bank{i}", [P, NC], F32)) for i in range(8)]

        def bank(b, *shape):
            if len(shape) == 2:
                return psum[b][:, 0:shape[0] * shape[1]].rearrange("p (a b) -> p a b", a=shape[0])
            return psum[b][:, :]

        at = [0]

        def stat(n):
            v = small[:, at[0]:at[0] + n]
            at[0] += n
            return v

        ssq, ms, ry, rt, lnv = stat(TT), stat(TT), stat(TT), stat(TT), stat(TT)
        nmax = stat(2 * NH)
        rsum, rinv = stat(2 * NH), stat(2 * NH)
        hm, hln, hy, ht = stat(2 * NH), stat(2 * NH), stat(2 * NH), stat(2 * NH)
        lba, lbb, lbc = stat(2 * NP), stat(2 * NP), stat(NP)
        logit, top, topf = stat(2 * NE), stat(2 * NE), stat(2 * NE)
        topi = small[:, at[0]:at[0] + 2 * NE].bitcast(U32)
        at[0] += 2 * NE
        oh1, oh2, selected = stat(2 * NE), stat(2 * NE), stat(2 * NE)
        gdiff, gexp, g1, g2 = stat(TT), stat(TT), stat(TT), stat(TT)
        table = stat(5 * NE).rearrange("p (a b) -> p a b", a=5)
        tprod = stat(5 * NE).rearrange("p (a b) -> p a b", a=5)
        items = stat(5 * (ITEMS + 1)).rearrange("p (a b) -> p a b", a=5)
        over, nover, hot = stat(NE), stat(NE), stat(NE)
        iitem = stat(4)
        assert at[0] <= 512

        filled = sems("filled", RING_SLOTS)
        tail_filled = sems("tail_filled", 3)
        consumed = sem("consumed")
        x_in = sem("x_in")
        vec_in = sem("vec_in")
        small_in = sem("small_in")
        wfg_in = sems("wfg_in", DEPTH)
        p_in = sems("p_in", DEPTH)
        fgain_in = sem("fgain_in")
        stored = sem("stored")
        consts = sem("consts")
        zeroed = sem("zeroed")
        vec_T = sem("vec_T")
        vec_ready = sem("vec_ready")
        dchain = sem("dchain")
        achain = sem("achain")
        NN = 3 * DEPTH + 1
        sq_done = sem("sq_done")
        ms_ready = sem("ms_ready")
        ry_ready = sem("ry_ready")
        un_ready = sem("un_ready")
        uT_psum = sem("uT_psum")
        uT_ready = sem("uT_ready")
        h_ready = {k: sem(f"h_ready{k}") for k in (1, 2, 3, 4, 6)}
        lb_max, lb_exp, lb_ready = sem("lb_max"), sem("lb_exp"), sem("lb_ready")
        proj = sems("proj", DEPTH)
        proj_a = sems("proj_a", DEPTH)
        proj_d = sems("proj_d", DEPTH)
        fg_abs, fg_exp, fg_ln, negc_ready = (sems(n, DEPTH) for n in ("fg_abs", "fg_exp", "fg_ln", "negc_ready"))
        en_ready, f_ready, logf_ready = (sems(n, DEPTH) for n in ("en_ready", "f_ready", "logf_ready"))
        arg_ready = sems("arg_ready", DEPTH)
        exp_ready = sems("exp_ready", DEPTH)
        xl_ready = sems("xl_ready", DEPTH)
        lev = sems("lev", DEPTH)
        lev_d = sems("lev_d", DEPTH)
        logits = sems("logits", DEPTH)
        nmax_ready = sems("nmax_ready", DEPTH)
        probs_ready = sems("probs_ready", DEPTH)
        pT_psum = sems("pT_psum", DEPTH)
        pT_ready = sems("pT_ready", DEPTH)
        hgrn_o = sems("hgrn_o", DEPTH)
        hgrn_c = sems("hgrn_c", DEPTH)
        fox_o = sems("fox_o", DEPTH)
        fox_n = sems("fox_n", DEPTH)
        hsq, hms, hry = (sems(n, DEPTH) for n in ("hsq", "hms", "hry"))
        mix_ready = sems("mix_ready", DEPTH)
        mT_psum, mT_ready = sems("mT_psum", DEPTH), sems("mT_ready", DEPTH)
        wo = sems("wo", DEPTH)
        ffu, ffsil, ffh_ready, ffd = (sem(n) for n in ("ffu", "ffsil", "ffh_ready", "ffd"))
        pT_ps, pT_rd = sems("ppT_psum", DEPTH), sems("ppT_ready", DEPTH)
        ple_p, ple_g, ple_sig, ple_prod = (sems(n, DEPTH) for n in ("ple_p", "ple_g", "ple_sig", "ple_prod"))
        rlog, rdiff, rexp, sel_count, ranks, table_ready = (sem(n) for n in ("rlog", "rdiff", "rexp", "sel_count", "ranks", "table_ready"))
        sel_ready, gath, uTe_ready, comb_ps, comb_ready = (sem(n) for n in ("sel_ready", "gath", "uTe_ready", "comb_ps", "comb_ready"))
        exg, exu, exsil, exh_ready, exT_ps, exT_ready = (sem(n) for n in ("exg", "exu", "exsil", "exh_ready", "exT_ps", "exT_ready"))
        y_done, y_a, y_d, comb, hacc, mchain = (sem(n) for n in ("y_done", "y_a", "y_d", "comb", "hacc", "mchain"))
        out_ready = sem("out_ready")


        def cols(w2, c0, n):
            return w2[:, c0:c0 + n].rearrange("(k p) n -> p k n", p=P)

        def chunk(kind, l, c):
            if kind == "in":
                return cols(w_in[l], COL[c], NC), KT * NC
            if kind == "out":
                return cols(w_out[l], c * NC, NC), KT * NC
            if kind in ("fg", "fu"):
                n = min(NC, DFF - c * NC)
                return cols((w_ffn_gate if kind == "fg" else w_ffn_up)[0], c * NC, n), KT * n
            if kind == "fd":
                n = min(NC, DFF - c * NC)
                return w_ffn_down[0, c * NC:c * NC + n, :].rearrange("(k p) n -> p k n", p=P), n // P * D
            if kind == "pe":
                return w_ple[l].rearrange("(k p) n -> p k n", p=P), PKT * D
            return cols(w_ple_gate[l], c * NC, NC), KT * NC

        def slot_view(s, n, k):
            return ring[:, s, 0:n].rearrange("p (k n) -> p k n", k=k)

        def where(key):
            n = STATIC.index(key)
            return n % RING_SLOTS, 16 * (n // RING_SLOTS + 1)

        FILL0 = [len([n for n in range(NSTATIC) if n % RING_SLOTS == s]) for s in range(RING_SLOTS)]

        def exp_slot(n):
            return (NSTATIC + n) % RING_SLOTS

        block = ctx.enter_context(nc.Block())

        @block.sync
        def _(sp):
            sp.dma_start(h[:, :, :], x[0].rearrange("(t p) d -> p t d", p=P)).then_inc(x_in, 16)

            for n, (kind, l, c) in enumerate(STATIC):
                src, size = chunk(kind, l, c)
                if n >= RING_SLOTS:
                    sp.wait_ge(consumed, n - RING_SLOTS + 1)
                s = n % RING_SLOTS
                sp.dma_start(slot_view(s, size, src.shape[1]), src).then_inc(filled[s], 16)

            sp.wait_ge(table_ready, 1)
            n_items = sp.value_load(item_expert[0:1, ITEMS:ITEMS + 1], min_val=NE, max_val=ITEMS)
            with sp.Fori(0, n_items) as i:
                e = sp.value_load(item_expert[0:1, bass.ds(i, 1)], min_val=0, max_val=NE - 1)
                for n, (kind, r) in enumerate(EXP_ORDER):
                    s = exp_slot(n)
                    sp.wait_ge(consumed, i * EXP_LOADS + (NSTATIC + n - RING_SLOTS + 1))
                    if kind == "d":
                        src = w_exp_down[0, bass.ds(e, 1), r * NC:(r + 1) * NC, :].rearrange("a (k p) n -> p (a k) n", p=P)
                    else:
                        w = w_exp_gate if kind == "g" else w_exp_up
                        src = w[0, bass.ds(e, 1), :, r * NC:(r + 1) * NC].rearrange("a (k p) n -> p (a k) n", p=P)
                    sp.dma_start(slot_view(s, SLOT, 4 if kind == "d" else KT), src).then_inc(filled[s], 16)
            for k, (kind, l, c) in enumerate(TAIL):
                src, size = chunk(kind, l, c)
                sp.wait_ge(consumed, n_items * EXP_LOADS + (NSTATIC + k - RING_SLOTS + 1))
                sp.dma_start(slot_view(exp_slot(k), size, src.shape[1]), src).then_inc(tail_filled[k], 16)

            for t in range(TT):
                sp.wait_ge(out_ready, t + 1)
                sp.dma_start(out[0, t * P:(t + 1) * P, :], fout[:, t, :]).then_inc(stored, 16)
            sp.wait_ge(stored, 16 * TT)

        @block.gpsimd
        def _(pool):
            nz = 0
            for t in (rows, ident, masks, before, pick, wfg, bias):
                v = t[:, :, :] if len(t.shape) == 3 else t[:, :]
                nc.gpsimd.memset(v, 0.0).then_inc(zeroed, 1)
                nz += 1
            nc.gpsimd.memset(scores[:, :, :, :], 0.0).then_inc(zeroed, 1)
            nc.gpsimd.memset(causal[:, :], 0.0).then_inc(zeroed, 1)
            nc.gpsimd.memset(ones[:, :], 1.0).then_inc(zeroed, 1)
            nz += 3
            assert nz == ZEROED
            nc.gpsimd.iota(iota[:, :], pattern=[[1, P]], base=0, channel_multiplier=0,
                           allow_small_or_imprecise_dtypes=True).then_inc(consts, 1)
            pool.wait_ge(zeroed, ZEROED)
            nc.gpsimd.affine_select(out=ident[:, :], in_=ident[:, :], compare_op=ALU.not_equal, fill=1.0,
                                    base=0, pattern=[[-1, P]], channel_multiplier=1).then_inc(consts, 1)
            nc.gpsimd.affine_select(out=causal[:, :], in_=causal[:, :], compare_op=ALU.is_ge, fill=NEG,
                                    base=0, pattern=[[-1, P]], channel_multiplier=1).then_inc(consts, 1)
            nc.gpsimd.affine_select(out=before[:, :], in_=before[:, :], compare_op=ALU.is_ge, fill=1.0,
                                    base=0, pattern=[[-1, P]], channel_multiplier=1).then_inc(consts, 1)
            nc.gpsimd.affine_select(out=pick[:, :, :], in_=pick[:, :, :], compare_op=ALU.not_equal, fill=1.0,
                                    base=0, pattern=[[-1, NH], [0, P]], channel_multiplier=1).then_inc(consts, 1)
            pool.wait_ge(consts, 5)
            nc.gpsimd.affine_select(out=pick[:, :, :], in_=pick[:, :, :], compare_op=ALU.not_equal, fill=1.0,
                                    base=-HD, pattern=[[-1, NH], [0, P]], channel_multiplier=1).then_inc(consts, 1)
            nc.gpsimd.affine_select(out=masks[:, NL - 1, :], in_=masks[:, NL - 1, :], compare_op=ALU.not_equal,
                                    fill=1.0, base=0, pattern=[[-1, P]], channel_multiplier=1).then_inc(consts, 1)
            done = 7
            for i, m in enumerate(LEVELS):
                nb = P // (2 * m)
                v = masks[:, i, :].rearrange("p (b u m) -> p b u m", u=2, m=m)[:, :, 1, :]
                nc.gpsimd.affine_select(out=v, in_=v, compare_op=ALU.is_ge, fill=1.0, base=-m,
                                        pattern=[[-2 * m, nb], [0, m]], channel_multiplier=1).then_inc(consts, 1)
                done += 1
                pool.wait_ge(consts, done)
                nc.gpsimd.affine_select(out=v, in_=v, compare_op=ALU.is_ge, fill=0.0, base=0,
                                        pattern=[[-2 * m, nb], [0, m]], channel_multiplier=1).then_inc(consts, 1)
                done += 1
            assert done == CONSTS

        @block.scalar
        def _(act):
            chain = [0]

            def link(ins):
                chain[0] += 1
                ins.then_inc(achain, 1)
                act.wait_ge(achain, chain[0])

            act.wait_ge(zeroed, ZEROED)
            for k, g in enumerate((mix_norm_gain, ffn_norm_gain, ple_norm_gain)):
                r0 = k * DEPTH * KT
                act.dma_start(rows[r0:r0 + DEPTH * KT, :], g.rearrange("l (k p) -> (l k) p", p=P)).then_inc(vec_in, 16)
            for l in range(DEPTH):
                r0 = ROW_OUT + l * KT
                act.dma_start(rows[r0:r0 + NP, :], fox_out_gain[l].rearrange("(k p) -> k p", p=P)).then_inc(vec_in, 16)
                act.dma_start(rows[r0 + NP:r0 + KT, :], hgrn_out_gain[l].rearrange("(k p) -> k p", p=P)).then_inc(vec_in, 16)
                act.dma_start(rows[ROW_LB + l * NP:ROW_LB + (l + 1) * NP, :],
                              hgrn_lb_logits[l].rearrange("(k p) -> k p", p=P)).then_inc(vec_in, 16)

            def load_wfg(l):
                src = cols(w_in[l], COL["fg"], NH)
                for c0 in (0, HD):
                    act.dma_start(wfg[:, :, c0:c0 + NH], src).then_inc(wfg_in[l], 16)

            def load_p(l):
                act.dma_start(pn[:, :, :], p[l, 0].rearrange("(t p) d -> p t d", p=P)).then_inc(p_in[l], 16)

            with nc.allow_non_contiguous_dma(reason="a few gate biases, one per partition"):
                for c0 in (0, HD):
                    act.dma_start(bias[c0:c0 + NH, :], fox_gate_bias.rearrange("l h -> h l")).then_inc(small_in, 16)
            load_wfg(0)
            act.dma_start(wr[:, :, :], w_router[0].rearrange("(k p) e -> p k e", p=P)).then_inc(small_in, 16)

            def inv_root(v, ln, y, ready, waits):
                act.wait_ge(*waits)
                link(nc.scalar.activation(ln, v, ACT.Ln))
                nc.scalar.activation(y, ln, ACT.Exp, scale=-0.5).then_inc(ready, 1)

            def norm(k, ready):
                for t in range(TT):
                    ready(t)
                    nc.scalar.activation(sqrow[t], h[:, t, :], ACT.Square, accum_out=ssq[:, t:t + 1]).then_inc(sq_done, 1)
                inv_root(ms, lnv, ry, ry_ready, (ms_ready, k + 1))

            def mixer(l):
                act.wait_ge(proj_d[l], 2)
                nc.scalar.activation(en, en, ACT.Exp, scale=-1.0).then_inc(en_ready[l], 1)
                for u in (2, 3):
                    act.wait_ge(proj[l], u + 1)
                    nc.scalar.activation(hqT[:, 2 * (u - 2):2 * (u - 2) + 2, :], bank(u % 4, 2, SEQ), ACT.Copy).then_inc(proj_a[l], 1)
                act.wait_ge(f_ready[l], 1)
                nc.scalar.activation(en, arg, ACT.Ln).then_inc(logf_ready[l], 1)
                act.wait_ge(fg_abs[l], 1)
                nc.scalar.activation(small_fg[1], small_fg[1], ACT.Exp).then_inc(fg_exp[l], 1)
                act.wait_ge(fg_exp[l], 1)
                nc.scalar.activation(small_fg[1], small_fg[1], ACT.Ln, bias=1.0).then_inc(fg_ln[l], 1)

                dest = [(qT, 0), (qT, 1), (kT, 0), (kT, 1), (fv, 0), (fv, 1), (hv, 0), (hv, 1), (hgate, 0), (hgate, 1)]
                for j, (to, c) in enumerate(dest):
                    u = 5 + j
                    act.wait_ge(proj[l], u + 1)
                    if to is qT or to is kT:
                        nc.scalar.activation(to[:, 2 * c:2 * c + 2, :], bank(u % 4, 2, SEQ), ACT.Copy,
                                             scale=HD ** -0.5 if to is qT else 1.0).then_inc(proj_a[l], 1)
                    else:
                        nc.scalar.activation(to[:, c, :], bank(u % 4), ACT.Silu if to is hgate else ACT.Copy).then_inc(proj_a[l], 1)
                    if j < len(LEVELS) + 1:
                        act.wait_ge(arg_ready[l], j + 1)
                        nc.scalar.activation(arg, arg, ACT.Exp).then_inc(exp_ready[l], 1)
                for u, unit in enumerate(UNITS):
                    act.wait_ge(nmax_ready[l], u + 1)
                    if u >= 2:
                        act.wait_ge(pT_psum[l], u - 1)
                    t, par, heads = unit
                    n = NC // len(heads)
                    for i, hd in enumerate(heads):
                        c = t * NH + hd
                        nc.scalar.activation(probs[u % 2][:, i * n:(i + 1) * n], bank(SBANK[u])[:, i * n:(i + 1) * n], ACT.Exp,
                                             bias=nmax[:, c:c + 1], accum_out=rsum[:, c:c + 1]).then_inc(probs_ready[l], 1)
                    if u == 0:
                        for tt in range(TT):
                            act.wait_ge(hgrn_o[l], tt + 1)
                            nc.scalar.activation(un[:, tt, W:2 * W], bank(2 + tt), ACT.Copy).then_inc(hgrn_c[l], 1)
                    if u >= 1:
                        pT_out(l, u - 1)
                pT_out(l, len(UNITS) - 1)
                for half in range(2):
                    c0 = W if half == 0 else 0
                    if half == 0:
                        act.wait_ge(hgrn_c[l], TT)
                    else:
                        act.wait_ge(fox_n[l], TT)
                        act.wait_ge(hms[l], 1)
                    nc.scalar.activation(sq, un[:, :, c0:c0 + W], ACT.Square).then_inc(hsq[l], 1)
                    inv_root(hm, hln, hy, hry[l], (hms[l], half + 1))

            def pT_out(l, u):
                act.wait_ge(pT_psum[l], u + 1)
                if u >= 2:
                    act.wait_ge(fox_o[l], u - 1)
                nc.scalar.activation(probsT[u % 2], bank(SBANK[u], 4, P), ACT.Copy).then_inc(pT_ready[l], 1)

            def ple(l, ready):
                act.wait_ge(pT_ps[l], 1)
                nc.scalar.activation(pT, bank(0, PKT, SEQ), ACT.Copy).then_inc(pT_rd[l], 1)
                norm(3 * l + 2, ready)
                for jj, j in enumerate(GORDER):
                    t, n = j // 2, j % 2
                    act.wait_ge(ple_g[l], jj + 1)
                    nc.scalar.activation(sig[:, t, n * NC:(n + 1) * NC], bank(4 + j), ACT.Sigmoid).then_inc(ple_sig[l], 1)

            act.wait_ge(lb_max, 1)
            nc.scalar.activation(lbb, lba, ACT.Exp).then_inc(lb_exp, 1)

            norm(0, lambda t: act.wait_ge(x_in, 16))
            mixer(0)
            norm(1, lambda t: act.wait_ge(h_ready[1], 2 * TT if t == 0 else 2 * TT))
            act.wait_ge(proj[0], 5)
            load_wfg(1)
            load_p(0)
            for j in range(DFF // P):
                act.wait_ge(ffu, j + 1)
                if j >= 2:
                    act.wait_ge(ffh_ready, j - 1)
                nc.scalar.activation(ffs[j % 2], bank(j % 4)[:, 0:SEQ], ACT.Silu).then_inc(ffsil, 1)
            ple(0, lambda t: act.wait_ge(h_ready[2], 2 * TT))
            norm(3, lambda t: act.wait_ge(h_ready[3], 2 * TT))
            mixer(1)
            norm(4, lambda t: act.wait_ge(h_ready[4], 2 * TT))
            load_p(1)
            act.wait_ge(rdiff, 1)
            nc.scalar.activation(gexp, gdiff, ACT.Exp).then_inc(rexp, 1)

            act.wait_ge(table_ready, 1)
            n_items = act.value_load(item_expert[0:1, ITEMS:ITEMS + 1], min_val=NE, max_val=ITEMS)
            with act.Fori(0, n_items) as i:
                act.wait_ge(comb_ps, i + 1)
                nc.scalar.activation(combT, bank(7)[:, 0:SEQ].rearrange("p (a b) -> p a b", a=TT), ACT.Copy).then_inc(comb_ready, 1)
                for r in range(EXR + 1):
                    if r < EXR:
                        act.wait_ge(exg, i * EXR + (r + 1))
                        nc.scalar.activation(exs[r % 2], bank(2 * (r % 2)), ACT.Silu).then_inc(exsil, 1)
                    if r >= 1:
                        act.wait_ge(exT_ps, i * EXR + r)
                        nc.scalar.activation(exhT[(r - 1) % 2], bank(4, 4, P), ACT.Copy).then_inc(exT_ready, 1)
                act.wait_ge(y_done, i + 1)
                nc.scalar.activation(ye[:, 0:NC], bank(5), ACT.Copy).then_inc(y_a, 1)
            act.wait_ge(hacc, n_items * 4 + 1)
            act.dma_start(fgain, final_norm_gain.rearrange("(a d) -> a d", a=1).to_broadcast([P, D])).then_inc(fgain_in, 16)
            ple(1, lambda t: None)
            norm(6, lambda t: act.wait_ge(h_ready[6], 2 * TT))

        @block.vector
        def _(dve):
            V = nc.vector
            chain = [0]

            def link(ins):
                chain[0] += 1
                ins.then_inc(dchain, 1)
                dve.wait_ge(dchain, chain[0])

            def refine(v, y, t):
                link(V.tensor_tensor(t, y, y, ALU.mult))
                link(V.tensor_tensor(t, t, v, ALU.mult))
                link(V.tensor_scalar(t, t, -0.5, 1.5, ALU.mult, ALU.add))
                link(V.tensor_tensor(y, y, t, ALU.mult))

            def norm_stats(k):
                dve.wait_ge(sq_done, k * TT + TT)
                V.tensor_scalar(ms, ssq, 1.0 / D, EPS, ALU.mult, ALU.add).then_inc(ms_ready, 1)
                dve.wait_ge(ms_ready, k + 1)
                dve.wait_ge(ry_ready, k + 1)
                refine(ms, ry, rt)

            def norm(k):
                norm_stats(k)
                for t in range(TT):
                    V.tensor_scalar(un[:, t, :], h[:, t, :], ry[:, t:t + 1], None, ALU.mult).then_inc(un_ready, 1)
                gains(k * 2 * TT, uT_psum, uT_ready, ROW_NORM(k))

            def gains(base, psum_sem, ready, row):
                for t in range(TT):
                    for q in range(2):
                        dve.wait_ge(psum_sem, base + 2 * t + q + 1)
                        g = vec[:, row + 4 * q:row + 4 * q + 4].unsqueeze(2).to_broadcast([P, 4, P])
                        V.tensor_tensor(uT[:, 4 * q:4 * q + 4, t * P:(t + 1) * P], bank(4 + 2 * t + q, 4, P), g,
                                        ALU.mult).then_inc(ready, 1)

            def add_h(unit_sem, order, banks, ready):
                for j, (t, n) in enumerate(order):
                    dve.wait_ge(unit_sem, j + 1)
                    hv_ = h[:, t, n * NC:(n + 1) * NC]
                    V.tensor_tensor(hv_, bank(banks[j]), hv_, ALU.add).then_inc(ready, 1)

            def halves(v, m):
                f = v.rearrange("p a b -> p (a b)").rearrange("p (b u m) -> p b u m", u=2, m=m)
                return f[:, :, 1, :], f[:, :, 0, :]

            def mixer(l):
                for u in range(2):
                    dve.wait_ge(proj[l], u + 1)
                    V.tensor_scalar(en[:, 2 * u:2 * u + 2, :], bank(u, 2, SEQ), GATE_FLOOR, None, ALU.max).then_inc(proj_d[l], 1)
                dve.wait_ge(en_ready[l], 1)
                link(V.tensor_scalar(arg, en, 1.0, None, ALU.add))
                link(V.reciprocal(arg, arg))
                link(V.tensor_tensor(keyT, en, arg, ALU.mult))
                for m in range(NP):
                    V.tensor_scalar(keyT[:, m, :], keyT[:, m, :], oml[:, l, m:m + 1], None, ALU.mult).then_inc(dchain, 1)
                    V.tensor_scalar(arg[:, m, :], arg[:, m, :], oml[:, l, m:m + 1], lb[:, l, m:m + 1], ALU.mult,
                                    ALU.add).then_inc(f_ready[l] if m == NP - 1 else dchain, 1)
                    chain[0] += 1 if m == NP - 1 else 2
                dve.wait_ge(proj[l], 5)
                link(V.tensor_scalar(small_fg[0], bank(0)[:, 0:SEQ], bias[:, l:l + 1], None, ALU.add))
                V.tensor_scalar(small_fg[1], small_fg[0], -1.0, None, ALU.mult).then_inc(dchain, 1)
                chain[0] += 1
                dve.wait_ge(dchain, chain[0])
                V.tensor_tensor(small_fg[1], small_fg[1], small_fg[0], ALU.min).then_inc(fg_abs[l], 1)
                dve.wait_ge(logf_ready[l], 1)
                for m in range(NP):
                    V.tensor_tensor_scan(bT[:, m, :], ones[:, :], en[:, m, :], 0.0, ALU.mult, ALU.add).then_inc(dchain, 1)
                    chain[0] += 1
                dve.wait_ge(fg_ln[l], 1)
                dve.wait_ge(dchain, chain[0])
                link(V.scalar_tensor_tensor(small_fg[0], small_fg[0], 0.0, small_fg[1], ALU.min, ALU.subtract))
                link(V.tensor_tensor_scan(small_fg[1], ones[:, :], small_fg[0], 0.0, ALU.mult, ALU.add))
                V.tensor_scalar(negc[:, :], small_fg[1], -1.0, None, ALU.mult).then_inc(negc_ready[l], 1)

                def args(i):
                    if i >= 1:
                        dve.wait_ge(xl_ready[l], 2 * i)
                    if i < len(LEVELS):
                        m = LEVELS[i]
                        bu, bl = halves(bT, m)
                        au, al = halves(arg, m)
                    else:
                        m = P
                        bu, bl = bT[:, :, P:SEQ], bT[:, :, 0:P]
                        au, al = arg[:, :, P:SEQ], arg[:, :, 0:P]
                    ref = bl[:, :, m - 1:m].to_broadcast(list(bl.shape))
                    V.tensor_tensor(au, bu, ref, ALU.subtract).then_inc(dchain, 1)
                    chain[0] += 1
                    V.tensor_tensor(al, ref, bl, ALU.subtract).then_inc(arg_ready[l], 1)

                def decayed(i):
                    dve.wait_ge(exp_ready[l], i + 1)
                    if i >= 2:
                        dve.wait_ge(lev[l], 4 * i)
                    if i < len(LEVELS):
                        m = LEVELS[i]
                        (qu, _), (_, kl), (au, al), (xu, xlo) = (halves(v, m) for v in (hqT, keyT, arg, xl[i % 2]))
                    else:
                        qu, kl = hqT[:, :, P:SEQ], keyT[:, :, 0:P]
                        au, al, xu, xlo = arg[:, :, P:SEQ], arg[:, :, 0:P], xl[i % 2][:, :, P:SEQ], xl[i % 2][:, :, 0:P]
                    V.tensor_tensor(xu, qu, au, ALU.mult).then_inc(xl_ready[l], 1)
                    V.tensor_tensor(xlo, kl, al, ALU.mult).then_inc(xl_ready[l], 1)

                def take(i):
                    for j in range(4):
                        t, par = j // 2, j % 2
                        dve.wait_ge(lev[l], 4 * i + j + 1)
                        mi = (i - 1) % NL
                        mask = masks[:, mi, :].bitcast(U32).unsqueeze(1).to_broadcast([P, NP, P])
                        V.copy_predicated(scores[:, t, par::2, :], mask, bank(4 + j, NP, P)).then_inc(lev_d[l], 1)

                args(0)
                dve.wait_ge(proj_a[l], 2)
                for i in range(len(LEVELS) + 1):
                    decayed(i)
                    if i < len(LEVELS):
                        args(i + 1)
                    take(i)
                for par in range(2):
                    dve.wait_ge(lev[l], 4 * NL + par + 1)
                    V.tensor_copy(cross[:, par::2, :], bank(4 + par, NP, P)).then_inc(lev_d[l], 1)

                for u, (t, par, heads) in enumerate(UNITS):
                    dve.wait_ge(logits[l], u + 1)
                    n = NC // len(heads)
                    s3 = bank(SBANK[u], len(heads), n)
                    cm = causal[:, :].unsqueeze(1).to_broadcast([P, len(heads), P])
                    link(V.tensor_tensor(s3[:, :, n - P:n], s3[:, :, n - P:n], cm, ALU.add))
                    c0 = t * NH + heads[0]
                    V.tensor_reduce(nmax[:, c0:c0 + 2 * len(heads) - 1:2], s3, AX, ALU.max, negate=True).then_inc(nmax_ready[l], 1)

                def head_norm(half):
                    c0 = W if half == 0 else 0
                    v = un[:, :, c0:c0 + W]
                    if half == 1:
                        dve.wait_ge(probs_ready[l], 2 * NH)
                        link(V.reciprocal(rinv, rsum))
                        for t in range(TT):
                            dve.wait_ge(fox_o[l], 2 if t == 0 else len(UNITS))
                            r = rinv[:, t * NH:(t + 1) * NH].unsqueeze(2).to_broadcast([P, NH, HD])
                            V.tensor_tensor(un[:, t, 0:W].rearrange("p (h d) -> p h d", h=NH), bank(2 + t, NH, HD), r,
                                            ALU.mult).then_inc(fox_n[l], 1)
                    dve.wait_ge(hsq[l], half + 1)
                    link(V.tensor_reduce(hm, sq.rearrange("p t (h d) -> p (t h) d", d=HD), AX, ALU.add))
                    V.tensor_scalar(hm, hm, 1.0 / HD, EPS, ALU.mult, ALU.add).then_inc(hms[l], 1)
                    dve.wait_ge(hms[l], half + 1)
                    dve.wait_ge(hry[l], half + 1)
                    refine(hm, hy, ht)
                    for t in range(TT):
                        vt = v[:, t, :].rearrange("p (h d) -> p h d", h=NH)
                        y = hy[:, t * NH:(t + 1) * NH].unsqueeze(2).to_broadcast([P, NH, HD])
                        if half == 0:
                            link(V.tensor_tensor(vt, vt, y, ALU.mult))
                            V.tensor_tensor(v[:, t, :], v[:, t, :], hgate[:, t, :], ALU.mult).then_inc(mix_ready[l], 1)
                        else:
                            if t == 0:
                                dve.wait_ge(fox_n[l], TT)
                            V.tensor_tensor(vt, vt, y, ALU.mult).then_inc(mix_ready[l], 1)

                dve.wait_ge(proj_a[l], 12)
                head_norm(0)
                head_norm(1)
                gains(0, mT_psum[l], mT_ready[l], ROW_OUT + l * KT)
                add_h(wo[l], [(0, 0), (1, 0), (0, 1), (1, 1)], [0, 1, 2, 3], h_ready[3 * l + 1])

            def ple(l):
                norm(3 * l + 2)
                for jj, j in enumerate(GORDER):
                    t, n = j // 2, j % 2
                    dve.wait_ge(ple_sig[l], jj + 1)
                    dve.wait_ge(ple_p[l], 4)
                    s = slice(n * NC, (n + 1) * NC)
                    link(V.tensor_tensor(prod[:, t, s], bank(j), sig[:, t, s], ALU.mult))
                    V.tensor_tensor(h[:, t, s], h[:, t, s], prod[:, t, s], ALU.add).then_inc(h_ready[3 * l + 3], 1)

            dve.wait_ge(vec_T, 1)
            V.tensor_copy(vec[:, :], bank(0)[:, 0:P]).then_inc(vec_ready, 1)
            dve.wait_ge(vec_ready, 1)
            l0, l1 = (vec[:, ROW_LB + l * NP:ROW_LB + (l + 1) * NP] for l in range(2))
            link(V.tensor_tensor(lbc, l0, l1, ALU.max))
            V.tensor_tensor(lba[:, 0:NP], l0, lbc, ALU.subtract).then_inc(dchain, 1)
            chain[0] += 1
            V.tensor_tensor(lba[:, NP:2 * NP], l1, lbc, ALU.subtract).then_inc(lb_max, 1)
            dve.wait_ge(lb_exp, 1)
            link(V.tensor_tensor(lbc, lbb[:, 0:NP], lbb[:, NP:2 * NP], ALU.add))
            link(V.reciprocal(lbc, lbc))
            link(V.memset(lb[:, 0, :], 0.0))
            link(V.tensor_tensor(lb[:, 1, :], lbb[:, NP:2 * NP], lbc, ALU.mult))
            link(V.tensor_scalar(oml[:, :, :], lb[:, :, :], -1.0, 1.0, ALU.mult, ALU.add))
            dve.wait_ge(small_in, 48)

            norm(0)
            mixer(0)
            norm(1)
            for j in range(DFF // P):
                dve.wait_ge(ffsil, j + 1)
                r, c = j // 4, j % 4
                V.tensor_tensor(ffh[r % 2][:, c, :], bank(j % 4)[:, SEQ:2 * SEQ], ffs[j % 2], ALU.mult).then_inc(ffh_ready, 1)
            for j in range(4):
                t, n = j // 2, j % 2
                dve.wait_ge(ffd, 1)
                hv_ = h[:, t, n * NC:(n + 1) * NC]
                V.tensor_tensor(hv_, bank(4 + j), hv_, ALU.add).then_inc(h_ready[2], 1)
            ple(0)
            norm(3)
            mixer(1)
            norm(4)

            dve.wait_ge(rlog, 1)
            link(V.tensor_copy(logit, bank(0)[:, 0:2 * NE]))
            for t in range(TT):
                c = slice(t * NE, (t + 1) * NE)
                link(V.max(top[:, c], logit[:, c]))
                link(V.max_index(topi[:, c], top[:, c], logit[:, c]))
            link(V.tensor_copy(topf, topi))
            t2 = top.rearrange("p (t e) -> p t e", t=TT)
            V.tensor_tensor(gdiff, t2[:, :, 1], t2[:, :, 0], ALU.subtract).then_inc(rdiff, 1)
            for t in range(TT):
                c = slice(t * NE, (t + 1) * NE)
                link(V.tensor_scalar(oh1[:, c], iota[:, 0:NE], topf[:, t * NE:t * NE + 1], None, ALU.is_equal))
                link(V.tensor_scalar(oh2[:, c], iota[:, 0:NE], topf[:, t * NE + 1:t * NE + 2], None, ALU.is_equal))
            V.tensor_tensor(selected, oh1, oh2, ALU.add).then_inc(sel_count, 1)
            dve.wait_ge(rexp, 1)
            link(V.tensor_scalar(g1, gexp, 1.0, None, ALU.add))
            link(V.reciprocal(g1, g1))
            link(V.tensor_tensor(g2, gexp, g1, ALU.mult))
            for t in range(TT):
                c = slice(t * NE, (t + 1) * NE)
                link(V.tensor_scalar(oh1[:, c], oh1[:, c], g1[:, t:t + 1], None, ALU.mult))
                link(V.scalar_tensor_tensor(table[:, 2 + t, :], oh2[:, c], g2[:, t:t + 1], oh1[:, c], ALU.mult, ALU.add))
            link(V.tensor_copy(table[:, 4, :], iota[:, 0:NE]))
            dve.wait_ge(ranks, 1)
            dve.wait_ge(sel_count, 1)
            for t in range(TT):
                c = slice(t * NE, (t + 1) * NE)
                link(V.scalar_tensor_tensor(table[:, t, :], bank(1)[:, c], 1.0, selected[:, c], ALU.add, ALU.mult))
                link(V.tensor_scalar(table[:, t, :], table[:, t, :], -1.0, None, ALU.add))
            link(V.tensor_scalar(over, bank(1)[:, 2 * NE:3 * NE], float(P), None, ALU.is_gt))
            link(V.tensor_tensor_scan(nover, ones[:, 0:NE], over, 0.0, ALU.mult, ALU.add))
            link(V.tensor_copy(items[:, :, 0:NE], table))
            for n in range(OVER):
                link(V.tensor_scalar(hot, nover, float(n + 1), None, ALU.is_equal))
                link(V.tensor_tensor(hot, hot, over, ALU.mult))
                link(V.tensor_tensor(tprod, table, hot.unsqueeze(1).to_broadcast([P, 5, NE]), ALU.mult))
                link(V.tensor_reduce(items[:, :, NE + n], tprod, AX, ALU.add))
            link(V.tensor_scalar(items[:, 0:2, NE:ITEMS], items[:, 0:2, NE:ITEMS], -float(P), None, ALU.add))
            V.tensor_scalar(items[:, 4, ITEMS:ITEMS + 1], nover[:, NE - 1:NE], float(NE), None, ALU.add).then_inc(hacc, 1)
            dve.wait_ge(hacc, 1)
            V.tensor_copy(item_expert[:, :], items[:, 4, :]).then_inc(table_ready, 1)
            dve.wait_ge(table_ready, 1)

            n_items = dve.value_load(item_expert[0:1, ITEMS:ITEMS + 1], min_val=NE, max_val=ITEMS)
            with dve.Fori(0, n_items) as i:
                V.tensor_scalar(iitem.unsqueeze(2), items[:, 0:4, bass.ds(i, 1)], 1.0, None, ALU.mult).then_inc(mchain, 1)
                dve.wait_ge(mchain, i * 3 + 1)
                for t in range(TT):
                    V.tensor_scalar(sel[:, t, :], iota[:, :], iitem[:, t:t + 1], None, ALU.is_equal).then_inc(mchain, 1)
                    dve.wait_ge(mchain, i * 3 + (t + 2))
                    V.tensor_scalar(selg[:, t, :], sel[:, t, :], iitem[:, 2 + t:3 + t], None, ALU.mult).then_inc(sel_ready, 1)
                for q in range(2):
                    dve.wait_ge(gath, i * 2 + (q + 1))
                    row = ROW_NORM(4) + 4 * q
                    g = vec[:, row:row + 4].unsqueeze(2).to_broadcast([P, 4, P])
                    V.tensor_tensor(uTe[:, 4 * q:4 * q + 4, :], bank(q, 4, P), g, ALU.mult).then_inc(uTe_ready, 1)
                for r in range(EXR):
                    dve.wait_ge(exsil, i * EXR + (r + 1))
                    dve.wait_ge(exu, i * EXR + (r + 1))
                    V.tensor_tensor(exh[r % 2], bank(2 * (r % 2) + 1), exs[r % 2], ALU.mult).then_inc(exh_ready, 1)
                dve.wait_ge(y_done, i + 1)
                V.tensor_copy(ye[:, NC:D], bank(6)).then_inc(y_d, 1)
                for j in range(4):
                    t, n = j // 2, j % 2
                    dve.wait_ge(comb, i * 4 + (j + 1))
                    hv_ = h[:, t, n * NC:(n + 1) * NC]
                    V.tensor_tensor(hv_, bank(j), hv_, ALU.add).then_inc(hacc, 1)
            dve.wait_ge(hacc, n_items * 4 + 1)
            ple(1)
            norm_stats(6)
            dve.wait_ge(fgain_in, 16)
            for t in range(TT):
                link(V.tensor_scalar(fout[:, t, :], h[:, t, :], ry[:, t:t + 1], None, ALU.mult))
                V.tensor_tensor(fout[:, t, :], fout[:, t, :], fgain, ALU.mult).then_inc(out_ready, 1)

        @block.tensor
        def _(pe):
            T = nc.tensor

            def norm(k):
                for t in range(TT):
                    pe.wait_ge(un_ready, k * TT + t + 1)
                    transposes(t, uT_psum)

            def transposes(t, done):
                for q in range(2):
                    for c in range(4):
                        last = T.transpose(bank(4 + 2 * t + q, 4, P)[:, c, :], un[:, t, (4 * q + c) * P:(4 * q + c + 1) * P], ident[:, :])
                    last.then_inc(done, 1)

            def arrived(key):
                s, v = where(key)
                pe.wait_ge(filled[s], v)
                kind, _, c = key
                if kind == "pe":
                    return slot_view(s, PKT * D, PKT)
                if kind == "fd":
                    n = min(NC, DFF - c * NC)
                    return slot_view(s, n // P * D, n // P)
                n = min(NC, DFF - c * NC) if kind in ("fg", "fu") else NC
                return slot_view(s, KT * n, KT)

            def mixer(l):
                unit = [0]

                def begin():
                    u = unit[0]
                    if u == 4:
                        pe.wait_ge(proj_d[l], 1)
                    elif u in (5,):
                        pe.wait_ge(proj_d[l], 2)
                    elif u in (6, 7):
                        pe.wait_ge(proj_a[l], u - 5)
                    elif u == 8:
                        pe.wait_ge(fg_abs[l], 1)
                    elif u >= 9:
                        pe.wait_ge(proj_a[l], u - 6)
                    unit[0] += 1
                    return u % 4

                def transposed(w, c, last_of_chunk):
                    b = begin()
                    o = bank(b, 2, SEQ)
                    for m in range(2):
                        col = (2 * c + m) * P
                        for k in range(KT):
                            last = T.matmul(o[:, m, :], w[:, k, col:col + P], uT[:, k, :], start=k == 0, stop=k == KT - 1)
                    finish(last, last_of_chunk)

                def natural(w, t, last_of_chunk):
                    b = begin()
                    for k in range(KT):
                        last = T.matmul(bank(b), uT[:, k, t * P:(t + 1) * P], w[:, k, :], start=k == 0, stop=k == KT - 1)
                    finish(last, last_of_chunk)

                def finish(last, last_of_chunk):
                    last.then_inc(proj[l], 1)
                    if last_of_chunk:
                        pe.wait_ge(proj[l], unit[0])
                        pe.sem_inc(consumed, 1)

                def level(i):
                    if i == 0:
                        pe.wait_ge(logf_ready[l], 1)
                        pe.wait_ge(proj_a[l], 2)
                    else:
                        pe.wait_ge(xl_ready[l], 2 * i)
                    if i >= 1:
                        pe.wait_ge(lev_d[l], 4 * i)
                    left, right = (keyT, hqT) if i == 0 else (xl[(i - 1) % 2], xl[(i - 1) % 2])
                    for t in range(TT if i < NL else 1):
                        for par in range(2):
                            b = bank(4 + 2 * t + par, NP, P)
                            r = slice(par * HD, (par + 1) * HD)
                            ts_, tt_ = (t, t) if i < NL else (0, 1)
                            for m in range(NP):
                                last = T.matmul(b[:, m, :], left[r, m, ts_ * P:(ts_ + 1) * P],
                                                right[r, m, tt_ * P:(tt_ + 1) * P], start=True, stop=True)
                            last.then_inc(lev[l], 1)

                w = arrived(("in", l, "hf"))
                for c in range(2):
                    transposed(w, c, c == 1)
                w = arrived(("in", l, "hq"))
                for c in range(2):
                    transposed(w, c, c == 1)
                pe.wait_ge(wfg_in[l], 32)
                b = begin()
                for k in range(KT):
                    last = T.matmul(bank(b)[:, 0:SEQ], wfg[:, k, :], uT[:, k, :], start=k == 0, stop=k == KT - 1)
                finish(last, False)
                grp = 0
                for name in IN_ORDER[2:]:
                    w = arrived(("in", l, name))
                    for c in range(2):
                        (transposed if name in ("fq", "fk") else natural)(w, c, c == 1)
                        if grp <= NL and (name != "fq" or c == 1):
                            level(grp)
                            grp += 1
                assert grp == NL + 1
                pe.wait_ge(negc_ready[l], 1)
                pe.wait_ge(proj_a[l], 6)
                for u, (t, par, heads) in enumerate(UNITS):
                    if u == 0:
                        pe.wait_ge(lev_d[l], 4 * NL + 2)
                    if u == 4:
                        pe.wait_ge(proj_a[l], 12)
                    n = NC // len(heads)
                    r = slice(par * HD, (par + 1) * HD)
                    for i, hd in enumerate(heads):
                        o = bank(SBANK[u])[:, i * n:(i + 1) * n]
                        T.matmul(o, qT[r, hd // 2, t * P:(t + 1) * P], kT[r, hd // 2, 0:n], start=True, stop=False)
                        last = T.matmul(o, pick[r, hd, :], negc[r, 0:n], start=False, stop=True)
                    last.then_inc(logits[l], 1)
                for t in range(TT):
                    for hd in range(NH):
                        o = bank(2 + t)[:, hd * HD:(hd + 1) * HD]
                        if t == 1:
                            T.matmul(o, cross[:, hd, :], hv[:, 0, hd * HD:(hd + 1) * HD], start=True, stop=False)
                        last = T.matmul(o, scores[:, t, hd, :], hv[:, t, hd * HD:(hd + 1) * HD], start=t == 0, stop=True)
                    last.then_inc(hgrn_o[l], 1)

                def attend(u):
                    t, par, heads = UNITS[u]
                    pe.wait_ge(pT_ready[l], u + 1)
                    if u == 0:
                        pe.wait_ge(hgrn_c[l], TT)
                    nk = t + 1
                    for i, hd in enumerate(heads):
                        for kt in range(nk):
                            last = T.matmul(bank(2 + t)[:, hd * HD:(hd + 1) * HD], probsT[u % 2][:, i * nk + kt, :],
                                            fv[:, kt, hd * HD:(hd + 1) * HD], start=kt == 0, stop=kt == nk - 1)
                    last.then_inc(fox_o[l], 1)

                ph = 0
                for u, (t, par, heads) in enumerate(UNITS):
                    ph += len(heads)
                    pe.wait_ge(probs_ready[l], ph)
                    for c in range(4):
                        last = T.transpose(bank(SBANK[u], 4, P)[:, c, :], probs[u % 2][:, c * P:(c + 1) * P], ident[:, :])
                    last.then_inc(pT_psum[l], 1)
                    if u >= 1:
                        attend(u - 1)
                attend(len(UNITS) - 1)
                pe.wait_ge(mix_ready[l], 2 * TT)
                for t in range(TT):
                    transposes(t, mT_psum[l])
                pe.wait_ge(mT_ready[l], 2 * TT)
                for n in range(2):
                    w = arrived(("out", l, n))
                    for t in range(TT):
                        for k in range(KT):
                            last = T.matmul(bank(2 * n + t), uT[:, k, t * P:(t + 1) * P], w[:, k, :], start=k == 0, stop=k == KT - 1)
                        last.then_inc(wo[l], 1)
                    pe.wait_ge(wo[l], 2 * n + 2)
                    pe.sem_inc(consumed, 1)

            def ple(l, gate_in):
                pe.wait_ge(p_in[l], 16)
                for t in range(TT):
                    for k in range(PKT):
                        last = T.transpose(bank(0, PKT, SEQ)[:, k, t * P:(t + 1) * P], pn[:, t, k * P:(k + 1) * P], ident[:, :])
                last.then_inc(pT_ps[l], 1)
                w = gate_in(0)
                pe.wait_ge(pT_rd[l], 1)
                for j in range(4):
                    t, n = j // 2, j % 2
                    for k in range(PKT):
                        last = T.matmul(bank(j), pT[:, k, t * P:(t + 1) * P], w[:, k, n * NC:(n + 1) * NC], start=k == 0, stop=k == PKT - 1)
                    last.then_inc(ple_p[l], 1)
                pe.wait_ge(ple_p[l], 4)
                pe.sem_inc(consumed, 1)
                norm(3 * l + 2)
                pe.wait_ge(uT_ready, (3 * l + 2) * 2 * TT + 4)
                for n in range(2):
                    w = gate_in(1 + n)
                    for t in range(TT):
                        for k in range(KT):
                            last = T.matmul(bank(4 + 2 * t + n), uT[:, k, t * P:(t + 1) * P], w[:, k, :], start=k == 0, stop=k == KT - 1)
                        last.then_inc(ple_g[l], 1)
                    pe.wait_ge(ple_g[l], 2 * n + 2)
                    pe.sem_inc(consumed, 1)

            pe.wait_ge(consts, CONSTS)
            pe.wait_ge(vec_in, 16 * (3 + 3 * DEPTH))
            T.transpose(bank(0)[:, 0:P], rows[:, :], ident[:, :]).then_inc(vec_T, 1)

            norm(0)
            pe.wait_ge(uT_ready, 0 * 2 * TT + 4)
            mixer(0)
            norm(1)
            pe.wait_ge(uT_ready, 1 * 2 * TT + 4)
            NF = DFF // P

            def down(j):
                r, c = j // 4, j % 4
                w = arrived(("fd", 0, r))
                pe.wait_ge(ffh_ready, j + 1)
                for t in range(TT):
                    for n in range(2):
                        last = T.matmul(bank(4 + 2 * t + n), ffh[r % 2][:, c, t * P:(t + 1) * P], w[:, c, n * NC:(n + 1) * NC],
                                        start=j == 0, stop=j == NF - 1)
                if j == NF - 1:
                    last.then_inc(ffd, 1)
                elif c == 3:
                    last.then_inc(consumed, 1)

            for j in range(NF):
                r, c = j // 4, j % 4
                wg, wu = arrived(("fg", 0, r)), arrived(("fu", 0, r))
                if j >= 4:
                    pe.wait_ge(ffh_ready, j - 3)
                for w, o in ((wg, 0), (wu, SEQ)):
                    for k in range(KT):
                        last = T.matmul(bank(j % 4)[:, o:o + SEQ], w[:, k, c * P:(c + 1) * P], uT[:, k, :], start=k == 0, stop=k == KT - 1)
                last.then_inc(ffu, 1)
                if c == 3 or j == NF - 1:
                    pe.wait_ge(ffu, j + 1)
                    pe.sem_inc(consumed, 2)
                if j >= 1:
                    down(j - 1)
            down(NF - 1)
            pe.wait_ge(ffd, 1)
            pe.sem_inc(consumed, 1)
            ple(0, lambda k: arrived([("pe", 0, 0), ("pg", 0, 0), ("pg", 0, 1)][k]))
            norm(3)
            pe.wait_ge(uT_ready, 3 * 2 * TT + 4)
            mixer(1)
            norm(4)
            pe.wait_ge(uT_ready, 4 * 2 * TT + 4)
            pe.wait_ge(small_in, 48)
            for t in range(TT):
                for k in range(KT):
                    last = T.matmul(bank(0)[:, t * NE:(t + 1) * NE], uT[:, k, t * P:(t + 1) * P], wr[:, k, :], start=k == 0, stop=k == KT - 1)
            last.then_inc(rlog, 1)
            pe.wait_ge(sel_count, 1)
            s0, s1 = selected[:, 0:NE], selected[:, NE:2 * NE]
            one = ones[:, 0:P]
            T.matmul(bank(1)[:, 0:NE], before[:, :], s0, start=True, stop=True)
            T.matmul(bank(1)[:, NE:2 * NE], one, s0, start=True, stop=False)
            T.matmul(bank(1)[:, NE:2 * NE], before[:, :], s1, start=False, stop=True)
            T.matmul(bank(1)[:, 2 * NE:3 * NE], one, s0, start=True, stop=False)
            T.matmul(bank(1)[:, 2 * NE:3 * NE], one, s1, start=False, stop=True).then_inc(ranks, 1)

            pe.wait_ge(table_ready, 1)
            n_items = pe.value_load(item_expert[0:1, ITEMS:ITEMS + 1], min_val=NE, max_val=ITEMS)
            with pe.Fori(0, n_items) as i:
                load_of = {kr: n for n, kr in enumerate(EXP_ORDER)}

                def chunk_in(kind, r):
                    n = load_of[(kind, r)]
                    s = exp_slot(n)
                    before_ = len([k for k in range(n) if exp_slot(k) == s])
                    pe.wait_ge(filled[s], i * (16 * EXP_LOADS // RING_SLOTS) + 16 * (FILL0[s] + before_ + 1))
                    return slot_view(s, SLOT, 4 if kind == "d" else KT)

                pe.wait_ge(sel_ready, i * 2 + 2)
                pe.wait_ge(hacc, i * 4 + 1)
                for q in range(2):
                    for c in range(4):
                        for t in range(TT):
                            k = 4 * q + c
                            last = T.matmul(bank(q, 4, P)[:, c, :], un[:, t, k * P:(k + 1) * P], sel[:, t, :], start=t == 0, stop=t == 1)
                    last.then_inc(gath, 1)
                for t in range(TT):
                    last = T.transpose(bank(7)[:, t * P:(t + 1) * P], selg[:, t, :], ident[:, :])
                last.then_inc(comb_ps, 1)
                pe.wait_ge(uTe_ready, i * 2 + 2)

                def turn(r):
                    pe.wait_ge(exh_ready, i * EXR + (r + 1))
                    for c in range(4):
                        last = T.transpose(bank(4, 4, P)[:, c, :], exh[r % 2][:, c * P:(c + 1) * P], ident[:, :])
                    last.then_inc(exT_ps, 1)

                def down_ex(r):
                    w = chunk_in("d", r)
                    pe.wait_ge(exT_ready, i * EXR + (r + 1))
                    for c in range(4):
                        for n in range(2):
                            last = T.matmul(bank(5 + n), exhT[r % 2][:, c, :], w[:, c, n * NC:(n + 1) * NC],
                                            start=r == 0 and c == 0, stop=r == EXR - 1 and c == 3)
                    return last

                for r in range(EXR):
                    w = chunk_in("g", r)
                    if r >= 2:
                        pe.wait_ge(exh_ready, i * EXR + (r - 1))
                    for k in range(KT):
                        last = T.matmul(bank(2 * (r % 2)), uTe[:, k, :], w[:, k, :], start=k == 0, stop=k == KT - 1)
                    last.then_inc(exg, 1)
                    if r >= 1:
                        turn(r - 1)
                    w = chunk_in("u", r)
                    for k in range(KT):
                        last = T.matmul(bank(2 * (r % 2) + 1), uTe[:, k, :], w[:, k, :], start=k == 0, stop=k == KT - 1)
                    last.then_inc(exu, 1)
                    pe.wait_ge(exu, i * EXR + (r + 1))
                    pe.sem_inc(consumed, 2)
                    if r >= 1:
                        down_ex(r - 1).then_inc(consumed, 1)
                turn(EXR - 1)
                down_ex(EXR - 1).then_inc(y_done, 1)
                pe.wait_ge(y_done, i + 1)
                pe.sem_inc(consumed, 1)
                pe.wait_ge(comb_ready, i + 1)
                pe.wait_ge(y_a, i + 1)
                pe.wait_ge(y_d, i + 1)
                for j in range(4):
                    t, n = j // 2, j % 2
                    T.matmul(bank(j), combT[:, t, :], ye[:, n * NC:(n + 1) * NC], start=True, stop=True).then_inc(comb, 1)

            def tail_in(k):
                pe.wait_ge(tail_filled[k], 16)
                n, kk = ((PKT * D, PKT) if k == 0 else (SLOT, KT))
                return slot_view(exp_slot(k), n, kk)

            pe.wait_ge(hacc, n_items * 4 + 1)
            ple(1, tail_in)


UNITS = [(0, 0, [0, 2, 4, 6]), (0, 1, [1, 3, 5, 7]),
         (1, 0, [0, 2]), (1, 1, [1, 3]), (1, 0, [4, 6]), (1, 1, [5, 7])]
SBANK = [4, 5, 6, 7, 0, 1]
GORDER = [0, 2, 1, 3]
ZEROED = 10
CONSTS = 7 + 2 * len(LEVELS)

_INS = ['x', 'p', 'w_in', 'fox_gate_bias', 'fox_out_gain', 'hgrn_lb_logits', 'hgrn_out_gain', 'w_out',
        'mix_norm_gain', 'ffn_norm_gain', 'ple_norm_gain', 'w_ffn_gate', 'w_ffn_up', 'w_ffn_down', 'w_router',
        'w_exp_gate', 'w_exp_up', 'w_exp_down', 'w_ple', 'w_ple_gate', 'final_norm_gain']
_OUTS = [((1, SEQ, D), 'float32')]


def kernel(**inputs):
    import numpy as _np
    import concourse.bacc as _bacc
    from concourse import mybir as _mybir
    from concourse.bass_utils import run_bass_kernel_spmd as _run

    nc = _bacc.Bacc("TRN2", target_bir_lowering=False, num_devices=1, dynamic_dma_scratch_size=2048)
    arrays, args = {}, []
    for name in _INS:
        a = _np.ascontiguousarray(inputs[name])
        arrays[f"in_{name}_dram"] = a
        args.append(nc.dram_tensor(f"in_{name}_dram", a.shape, _mybir.dt.from_np(a.dtype), kind="ExternalInput").ap())
    for i, (shape, dtype) in enumerate(_OUTS):
        dt = _mybir.dt.from_np(_np.dtype(dtype))
        args.append(nc.dram_tensor(f"out_{i}_dram", shape, dt, kind="ExternalOutput").ap())
    trunk(nc, *args)
    r = _run(nc, [arrays], core_ids=[0])
    got = tuple(r.results[0][f"out_{i}_dram"] for i in range(len(_OUTS)))
    return got[0]
```

```python
from contextlib import ExitStack

import concourse.bass as bass
from concourse import mybir

P = 128
DEPTH = 2
SEQ = 256
TT = SEQ // P
D = 1024
KT = D // P
DPLE = 256
PKT = DPLE // P
HD = 64
NH = 8
W = NH * HD
NP = NH // 2
DIN = 7 * W + NH
DFF = 2816
NE = 8
DEX = 3584
NC = 512
HALF = KT // 2
CHUNK = HALF * NC
RAW = 7
SPLIT = 3
FFR = (DFF + NC - 1) // NC
EXR = DEX // NC
OVER = (2 * SEQ) // (P + 1)
ITEMS = NE + OVER
EPS = 1e-6
NEG = -1.0e30
GATE_FLOOR = -80.0
LEVELS = [1, 2, 4, 8, 16, 32, 64]
NL = len(LEVELS) + 1

ALU = mybir.AluOpType
ACT = mybir.ActivationFunctionType
F32 = mybir.dt.float32
F32R = mybir.dt.float32r
I32 = mybir.dt.int32
U32 = mybir.dt.uint32
AX = mybir.AxisListType.X

COL = dict(fq=0, fk=W, fv=2 * W, fg=3 * W, hq=3 * W + NH, hf=4 * W + NH, hi=5 * W + NH, hg=6 * W + NH)
IN_ORDER = ["hf", "hq", "fq", "fk", "fv", "hi", "hg"]
IN_TRANSPOSED = IN_ORDER[0:4]

ROW_NORM = lambda k: (k % 3) * DEPTH * KT + (k // 3) * KT
ROW_OUT = 3 * DEPTH * KT
ROW_LB = ROW_OUT + DEPTH * KT
ROWS = ROW_LB + DEPTH * NP

EXP_ORDER = [("g", 0, 0), ("g", 0, 1), ("u", 0, 0), ("u", 0, 1)]
for _r in range(1, EXR):
    EXP_ORDER += [(_k, _c, _h) for _k, _c in (("g", _r), ("d", _r - 1), ("u", _r)) for _h in range(2)]
EXP_ORDER += [("d", EXR - 1, 0), ("d", EXR - 1, 1)]
EXP_LOADS = len(EXP_ORDER)
LO_DVE = 1408
assert EXP_LOADS % RAW == 0 and EXP_LOADS % SPLIT == 0


def ff_halves(r):
    return 2 if DFF - r * NC >= NC else 1


def static_chunks():
    order = []
    for l in range(DEPTH):
        order += [("in", l, c, hf) for c in IN_ORDER for hf in range(2)]
        order += [("out", l, n, hf) for n in range(2) for hf in range(2)]
        if l == 0:
            for r in range(FFR):
                order += [("fg", l, r, hf) for hf in range(ff_halves(r))]
                if r >= 1:
                    order += [("fd", l, r - 1, hf) for hf in range(ff_halves(r - 1))]
                order += [("fu", l, r, hf) for hf in range(ff_halves(r))]
            order += [("fd", l, FFR - 1, hf) for hf in range(ff_halves(FFR - 1))]
            order += ple_chunks(l)
    return order


def ple_chunks(l):
    return [("pe", l, 0, 0)] + [("pg", l, n, hf) for n in range(2) for hf in range(2)]


STATIC = static_chunks()
NSTATIC = len(STATIC)
TAIL = ple_chunks(1)
TURN_NORM = [0, 2, 3, 4, 6, 7]
TURN_MIX = [1, 5]


def done(key):
    return STATIC.index(key) + 1


def trunk(nc, x, p, w_in, fox_gate_bias, fox_out_gain, hgrn_lb_logits, hgrn_out_gain, w_out,
          mix_norm_gain, ffn_norm_gain, ple_norm_gain, w_ffn_gate, w_ffn_up, w_ffn_down, w_router,
          w_exp_gate, w_exp_up, w_exp_down, w_ple, w_ple_gate, final_norm_gain, out):
    ctx = ExitStack()
    with ctx:
        def sb(name, shape, dt=F32):
            return ctx.enter_context(nc.sbuf_tensor(name, shape, dt))

        def sem(name):
            return ctx.enter_context(nc.semaphore(name))

        def sems(name, n):
            return [sem(f"{name}{i}") for i in range(n)]

        raw = sb("raw", [P, RAW, CHUNK])
        whi = sb("whi", [P, SPLIT, CHUNK], F32R)
        wlo = sb("wlo", [P, SPLIT, CHUNK], F32R)
        h = sb("h", [P, TT, D])
        un = sb("un", [P, TT, D])
        uTh = sb("uTh", [P, KT, SEQ], F32R)
        uTl = sb("uTl", [P, KT, SEQ], F32R)
        hTr = sb("hTr", [P, 2, TT * NC], F32R)
        work = sb("work", [P, 12 * 1024])
        scores = sb("scores", [P, TT, NH, P])
        vec = sb("vec", [P, P])
        rows = sb("rows", [P, P])
        ident = sb("ident", [P, P])
        masks = sb("masks", [P, NL, P])
        causal = sb("causal", [P, P])
        before = sb("before", [P, P])
        ones = sb("ones", [P, SEQ])
        pick = sb("pick", [P, NH, P])
        wfg = sb("wfg", [P, KT, P])
        bias = sb("bias", [P, DEPTH])
        wr = sb("wr", [P, KT, NE])
        iota = sb("iota", [P, P])
        lb = sb("lb", [P, DEPTH, NP])
        oml = sb("oml", [P, DEPTH, NP])
        small = sb("small", [P, 512])
        item_expert = sb("item_expert", [P, ITEMS + 1], I32)
        negc = sb("negc", [P, SEQ])
        fgt = sb("fgt", [P, 2, SEQ])
        small_fg = [fgt[:, i, :] for i in range(2)]

        def region(at, *shape):
            n = 1
            for s in shape:
                n *= s
            v = work[:, at:at + n]
            if len(shape) == 2:
                return v.rearrange("p (a b) -> p a b", a=shape[0])
            if len(shape) == 3:
                return v.rearrange("p (a b c) -> p a b c", a=shape[0], b=shape[1])
            return v

        qT = region(0, NP, SEQ)
        kT = region(1024, NP, SEQ)
        fv = region(2048, TT, W)
        hqT = region(3072, NP, SEQ)
        hv = region(4096, TT, W)
        hgate = region(5120, TT, W)
        en = region(6144, NP, SEQ)
        cross = region(6144, NH, P)
        keyT = region(7168, NP, SEQ)
        bT = region(8192, NP, SEQ)
        arg = region(9216, NP, SEQ)
        xl = [region(10240 + 1024 * i, NP, SEQ) for i in range(2)]
        probs = [region(10240 + 512 * i, NC) for i in range(2)]
        probsT = [region(11264 + 512 * i, 4, P) for i in range(2)]
        sq = region(9216, TT, W)
        uT = region(10240, KT, SEQ)
        sqrow = [region(9216 + D * t, D) for t in range(TT)]
        ffs = [region(512 * t, NC) for t in range(TT)]
        ffh = [region(1024 + 512 * t, NC) for t in range(TT)]
        ffT = [hTr[:, i, :].rearrange("p (t c n) -> p t c n", t=TT, c=4) for i in range(2)]
        pn = region(8192, TT, DPLE)
        pT = [hTr[:, i, 0:PKT * SEQ].rearrange("p (k n) -> p k n", k=PKT) for i in range(2)]
        sig = region(4096, TT, D)
        prod = region(6144, TT, D)
        uTe = region(0, KT, P)
        exs = [region(1024 + 512 * i, NC) for i in range(2)]
        exh = [region(2048 + 512 * i, NC) for i in range(2)]
        uTeh, uTel = uTh[:, :, 0:P], uTl[:, :, 0:P]
        exhT = [hTr[:, i, 0:NC].rearrange("p (c n) -> p c n", c=4) for i in range(2)]
        ye = region(4096, D)
        sel = region(5120, TT, P)
        selg = region(5376, TT, P)
        combT = region(5632, TT, P)
        fgain = region(0, D)
        fout = region(1024, TT, D)

        psum = [ctx.enter_context(nc.psum_tensor(f"bank{i}", [P, NC], F32)) for i in range(8)]

        def bank(b, *shape):
            if len(shape) == 2:
                return psum[b][:, 0:shape[0] * shape[1]].rearrange("p (a b) -> p a b", a=shape[0])
            return psum[b][:, :]

        at = [0]

        def stat(n):
            v = small[:, at[0]:at[0] + n]
            at[0] += n
            return v

        ssq, ms, ry, rt = stat(TT), stat(TT), stat(TT), stat(TT)
        nmax = stat(2 * NH)
        rsum, rinv = stat(2 * NH), stat(2 * NH)
        hm, hy, ht = stat(2 * NH), stat(2 * NH), stat(2 * NH)
        lba, lbb, lbc = stat(2 * NP), stat(2 * NP), stat(NP)
        logit, top, topf = stat(2 * NE), stat(2 * NE), stat(2 * NE)
        topi = small[:, at[0]:at[0] + 2 * NE].bitcast(U32)
        at[0] += 2 * NE
        oh1, oh2, selected = stat(2 * NE), stat(2 * NE), stat(2 * NE)
        gdiff, gexp, g1, g2 = stat(TT), stat(TT), stat(TT), stat(TT)
        table = stat(5 * NE).rearrange("p (a b) -> p a b", a=5)
        tprod = stat(5 * NE).rearrange("p (a b) -> p a b", a=5)
        items = stat(5 * (ITEMS + 1)).rearrange("p (a b) -> p a b", a=5)
        over, nover, hot = stat(NE), stat(NE), stat(NE)
        iitem = stat(4)
        assert at[0] <= 512

        filled = sems("filled", RAW)
        hi_a = sem("hi_a")
        lo_s = sem("lo_s")
        lo_p, lo_d = sem("lo_p"), sem("lo_d")
        y_half = sem("y_half")
        consumed = sem("consumed")
        x_in = sem("x_in")
        vec_in = sem("vec_in")
        small_in = sem("small_in")
        wfg_in = sems("wfg_in", DEPTH)
        p_in = sems("p_in", DEPTH)
        fgain_in = sem("fgain_in")
        stored = sem("stored")
        consts = sem("consts")
        zeroed = sem("zeroed")
        vec_T = sem("vec_T")
        vec_ready = sem("vec_ready")
        dchain = sem("dchain")
        NN = 3 * DEPTH + 1
        sq_done = sem("sq_done")
        ms_ready = sem("ms_ready")
        ry_ready = sem("ry_ready")
        un_ready = sem("un_ready")
        uT_psum = sem("uT_psum")
        tmp_ready = sem("tmp_ready")
        uh_ready = sem("uh_ready")
        uT_ready = sem("uT_ready")
        h_ready = {k: sem(f"h_ready{k}") for k in (1, 2, 3, 4, 6)}
        lb_max, lb_exp, lb_ready = sem("lb_max"), sem("lb_exp"), sem("lb_ready")
        fgp = sems("fgp", DEPTH)
        proj_a = sems("proj_a", DEPTH)
        proj_d = sems("proj_d", DEPTH)
        fg_abs, fg_exp, fg_ln, negc_ready = (sems(n, DEPTH) for n in ("fg_abs", "fg_exp", "fg_ln", "negc_ready"))
        en_ready, f_ready, logf_ready = (sems(n, DEPTH) for n in ("en_ready", "f_ready", "logf_ready"))
        arg_ready = sems("arg_ready", DEPTH)
        exp_ready = sems("exp_ready", DEPTH)
        xl_ready = sems("xl_ready", DEPTH)
        lev = sems("lev", DEPTH)
        lev_d = sems("lev_d", DEPTH)
        logits = sems("logits", DEPTH)
        nmax_ready = sems("nmax_ready", DEPTH)
        probs_ready = sems("probs_ready", DEPTH)
        pT_psum = sems("pT_psum", DEPTH)
        pT_ready = sems("pT_ready", DEPTH)
        hgrn_o = sems("hgrn_o", DEPTH)
        hgrn_c = sems("hgrn_c", DEPTH)
        fox_o = sems("fox_o", DEPTH)
        fox_n = sems("fox_n", DEPTH)
        hsq, hms, hry = (sems(n, DEPTH) for n in ("hsq", "hms", "hry"))
        mix_ready = sems("mix_ready", DEPTH)
        ffsil, ffh_ready, ffT_ps, ffT_hi, ffT_ready = (sem(n) for n in ("ffsil", "ffh_ready", "ffT_ps", "ffT_hi", "ffT_ready"))
        pT_ps, pT_hi, pT_rd, ple_sig = (sems(n, DEPTH) for n in ("ppT_psum", "ppT_hi", "ppT_ready", "ple_sig"))
        rlog, rdiff, rexp, sel_count, ranks, table_ready = (sem(n) for n in ("rlog", "rdiff", "rexp", "sel_count", "ranks", "table_ready"))
        sel_ready, gath, etmp_ready, euh_ready, uTe_ready, comb_ps, comb_ready = (sem(n) for n in (
            "sel_ready", "gath", "etmp_ready", "euh_ready", "uTe_ready", "comb_ps", "comb_ready"))
        exsil, exh_ready, exT_ps, exT_hi, exT_ready = (sem(n) for n in ("exsil", "exh_ready", "exT_ps", "exT_hi", "exT_ready"))
        y_a, y_d, comb, hacc, mchain = (sem(n) for n in ("y_a", "y_d", "comb", "hacc", "mchain"))
        out_ready = sem("out_ready")


        def rows_of(w2, k0, nk, c0, n):
            return w2[k0 * P:(k0 + nk) * P, c0:c0 + n].rearrange("(k p) n -> p k n", p=P)

        def source(key):
            kind, l, c, hf = key
            if kind == "in" and c in IN_TRANSPOSED:
                return rows_of(w_in[l], 0, KT, COL[c] + hf * NC // 2, NC // 2)
            if kind == "in":
                return rows_of(w_in[l], hf * HALF, HALF, COL[c], NC)
            if kind == "out":
                return rows_of(w_out[l], hf * HALF, HALF, c * NC, NC)
            if kind in ("fg", "fu"):
                w = (w_ffn_gate if kind == "fg" else w_ffn_up)[0]
                if ff_halves(c) == 1:
                    return rows_of(w, 0, KT, c * NC, NC // 2)
                return rows_of(w, hf * HALF, HALF, c * NC, NC)
            if kind == "fd":
                return rows_of(w_ffn_down[0], 4 * c + 2 * hf, 2, 0, D)
            if kind == "pe":
                return rows_of(w_ple[l], 0, PKT, 0, D)
            return rows_of(w_ple_gate[l], hf * HALF, HALF, c * NC, NC)

        def as_k(v, k):
            return v.rearrange("p (k n) -> p k n", k=k)

        def fills(n):
            return n // RAW + 1

        def exp_filled(n, i):
            return filled[(NSTATIC + n) % RAW], i * (16 * EXP_LOADS // RAW) + 16 * fills(NSTATIC + n)

        def lo_part(engine, n, c0=0, c1=CHUNK):
            return engine.tensor_tensor(wlo[:, n % SPLIT, c0:c1], raw[:, n % RAW, c0:c1],
                                        whi[:, n % SPLIT, c0:c1].bitcast(F32), ALU.subtract)

        block = ctx.enter_context(nc.Block())

        @block.sync
        def _(sp):
            sp.dma_start(h[:, :, :], x[0].rearrange("(t p) d -> p t d", p=P)).then_inc(x_in, 16)
            sp.wait_ge(zeroed, 3)
            for k, g in enumerate((mix_norm_gain, ffn_norm_gain, ple_norm_gain)):
                r0 = k * DEPTH * KT
                sp.dma_start(rows[r0:r0 + DEPTH * KT, :], g.rearrange("l (k p) -> (l k) p", p=P)).then_inc(vec_in, 16)
            for l in range(DEPTH):
                r0 = ROW_OUT + l * KT
                sp.dma_start(rows[r0:r0 + NP, :], fox_out_gain[l].rearrange("(k p) -> k p", p=P)).then_inc(vec_in, 16)
                sp.dma_start(rows[r0 + NP:r0 + KT, :], hgrn_out_gain[l].rearrange("(k p) -> k p", p=P)).then_inc(vec_in, 16)
                sp.dma_start(rows[ROW_LB + l * NP:ROW_LB + (l + 1) * NP, :],
                             hgrn_lb_logits[l].rearrange("(k p) -> k p", p=P)).then_inc(vec_in, 16)

            for n, key in enumerate(STATIC):
                src = source(key)
                if n >= RAW:
                    sp.wait_ge(consumed, n - RAW + 1)
                sp.dma_start(as_k(raw[:, n % RAW, :], src.shape[1]), src).then_inc(filled[n % RAW], 16)

            sp.wait_ge(table_ready, 1)
            n_items = sp.value_load(item_expert[0:1, ITEMS:ITEMS + 1], min_val=NE, max_val=ITEMS)
            with sp.Fori(0, n_items) as i:
                e = sp.value_load(item_expert[0:1, bass.ds(i, 1)], min_val=0, max_val=NE - 1)
                for n, (kind, r, hf) in enumerate(EXP_ORDER):
                    sp.wait_ge(consumed, i * EXP_LOADS + (NSTATIC + n - RAW + 1))
                    if kind == "d":
                        r0 = r * NC + hf * 2 * P
                        src = w_exp_down[0, bass.ds(e, 1), r0:r0 + 2 * P, :]
                    else:
                        w = w_exp_gate if kind == "g" else w_exp_up
                        src = w[0, bass.ds(e, 1), hf * HALF * P:(hf + 1) * HALF * P, r * NC:(r + 1) * NC]
                    s = (NSTATIC + n) % RAW
                    sp.dma_start(as_k(raw[:, s, :], 2 if kind == "d" else HALF),
                                 src.rearrange("a (k p) n -> p (a k) n", p=P)).then_inc(filled[s], 16)
            for k, key in enumerate(TAIL):
                src = source(key)
                sp.wait_ge(consumed, n_items * EXP_LOADS + (NSTATIC - RAW + k + 1))
                sp.dma_start(as_k(raw[:, (NSTATIC + k) % RAW, :], src.shape[1]), src).then_inc(filled[(NSTATIC + k) % RAW], 16)

            for t in range(TT):
                sp.wait_ge(out_ready, t + 1)
                sp.dma_start(out[0, t * P:(t + 1) * P, :], fout[:, t, :]).then_inc(stored, 16)
            sp.wait_ge(stored, 16 * TT)

        @block.gpsimd
        def _(pool):
            nz = 0
            for t in (rows, wfg, bias, ident, masks, before, pick):
                v = t[:, :, :] if len(t.shape) == 3 else t[:, :]
                nc.gpsimd.memset(v, 0.0).then_inc(zeroed, 1)
                nz += 1
            nc.gpsimd.memset(scores[:, :, :, :], 0.0).then_inc(zeroed, 1)
            nc.gpsimd.memset(causal[:, :], 0.0).then_inc(zeroed, 1)
            nc.gpsimd.memset(ones[:, :], 1.0).then_inc(zeroed, 1)
            nz += 3
            assert nz == ZEROED
            nc.gpsimd.iota(iota[:, :], pattern=[[1, P]], base=0, channel_multiplier=0,
                           allow_small_or_imprecise_dtypes=True).then_inc(consts, 1)
            pool.wait_ge(zeroed, ZEROED)
            nc.gpsimd.affine_select(out=ident[:, :], in_=ident[:, :], compare_op=ALU.not_equal, fill=1.0,
                                    base=0, pattern=[[-1, P]], channel_multiplier=1).then_inc(consts, 1)
            nc.gpsimd.affine_select(out=causal[:, :], in_=causal[:, :], compare_op=ALU.is_ge, fill=NEG,
                                    base=0, pattern=[[-1, P]], channel_multiplier=1).then_inc(consts, 1)
            nc.gpsimd.affine_select(out=before[:, :], in_=before[:, :], compare_op=ALU.is_ge, fill=1.0,
                                    base=0, pattern=[[-1, P]], channel_multiplier=1).then_inc(consts, 1)
            nc.gpsimd.affine_select(out=pick[:, :, :], in_=pick[:, :, :], compare_op=ALU.not_equal, fill=1.0,
                                    base=0, pattern=[[-1, NH], [0, P]], channel_multiplier=1).then_inc(consts, 1)
            pool.wait_ge(consts, 5)
            nc.gpsimd.affine_select(out=pick[:, :, :], in_=pick[:, :, :], compare_op=ALU.not_equal, fill=1.0,
                                    base=-HD, pattern=[[-1, NH], [0, P]], channel_multiplier=1).then_inc(consts, 1)
            nc.gpsimd.affine_select(out=masks[:, NL - 1, :], in_=masks[:, NL - 1, :], compare_op=ALU.not_equal,
                                    fill=1.0, base=0, pattern=[[-1, P]], channel_multiplier=1).then_inc(consts, 1)
            built = 7
            for i, m in enumerate(LEVELS):
                nb = P // (2 * m)
                v = masks[:, i, :].rearrange("p (b u m) -> p b u m", u=2, m=m)[:, :, 1, :]
                nc.gpsimd.affine_select(out=v, in_=v, compare_op=ALU.is_ge, fill=1.0, base=-m,
                                        pattern=[[-2 * m, nb], [0, m]], channel_multiplier=1).then_inc(consts, 1)
                built += 1
                pool.wait_ge(consts, built)
                nc.gpsimd.affine_select(out=v, in_=v, compare_op=ALU.is_ge, fill=0.0, base=0,
                                        pattern=[[-2 * m, nb], [0, m]], channel_multiplier=1).then_inc(consts, 1)
                built += 1
            assert built == CONSTS

            for n in range(NSTATIC):
                pool.wait_ge(hi_a, n + 1)
                lo_part(nc.gpsimd, n).then_inc(lo_s, 1)
            pool.wait_ge(table_ready, 1)
            n_items = pool.value_load(item_expert[0:1, ITEMS:ITEMS + 1], min_val=NE, max_val=ITEMS)
            with pool.Fori(0, n_items) as i:
                for n in range(EXP_LOADS):
                    pool.wait_ge(hi_a, i * EXP_LOADS + (NSTATIC + n + 1))
                    lo_part(nc.gpsimd, NSTATIC + n, LO_DVE).then_inc(lo_p, 1)
            for k in range(len(TAIL)):
                pool.wait_ge(hi_a, n_items * EXP_LOADS + (NSTATIC + k + 1))
                lo_part(nc.gpsimd, NSTATIC + k, LO_DVE).then_inc(lo_p, 1)

        @block.scalar
        def _(act):
            act.wait_ge(zeroed, 3)
            def load_wfg(l):
                src = rows_of(w_in[l], 0, KT, COL["fg"], NH)
                for c0 in (0, HD):
                    act.dma_start(wfg[:, :, c0:c0 + NH], src).then_inc(wfg_in[l], 16)

            def load_p(l):
                act.dma_start(pn[:, :, :], p[l, 0].rearrange("(t p) d -> p t d", p=P)).then_inc(p_in[l], 16)

            with nc.allow_non_contiguous_dma(reason="a few gate biases, one per partition"):
                for c0 in (0, HD):
                    act.dma_start(bias[c0:c0 + NH, :], fox_gate_bias.rearrange("l h -> h l")).then_inc(small_in, 16)
            load_wfg(0)
            act.dma_start(wr[:, :, :], w_router[0].rearrange("(k p) e -> p k e", p=P)).then_inc(small_in, 16)

            def root(v, y, ready, waits):
                act.wait_ge(*waits)
                nc.scalar.activation(y, v, ACT.Sqrt).then_inc(ready, 1)

            def norm(k, ready, c):
                hi_upto(c + 2)
                for t in range(TT):
                    ready(t)
                    nc.scalar.activation(sqrow[t], h[:, t, :], ACT.Square, accum_out=ssq[:, t:t + 1]).then_inc(sq_done, 1)
                root(ms, ry, ry_ready, (ms_ready, k + 1))
                if k < 3 * DEPTH:
                    hi_parts(TURN_NORM[k])

            ahead = [0]

            def hi_upto(m):
                while ahead[0] <= min(m, NSTATIC - 1):
                    n = ahead[0]
                    act.wait_ge(filled[n % RAW], 16 * fills(n))
                    if n >= SPLIT:
                        act.wait_ge(consumed, n - SPLIT + 1)
                    nc.scalar.activation(whi[:, n % SPLIT, :], raw[:, n % RAW, :], ACT.Copy).then_inc(hi_a, 1)
                    ahead[0] += 1

            def hi_parts(turn):
                for j in range(2 * TT):
                    t, q = j // 2, j % 2
                    act.wait_ge(tmp_ready, 4 * turn + j + 1)
                    s = slice(t * P, (t + 1) * P)
                    nc.scalar.activation(uTh[:, 4 * q:4 * q + 4, s], uT[:, 4 * q:4 * q + 4, s], ACT.Copy).then_inc(uh_ready, 1)

            def mixer(l):
                first = STATIC.index(("in", l, "hf", 0))
                hi_upto(first + 3)
                act.wait_ge(proj_d[l], 2)
                nc.scalar.activation(en, en, ACT.Exp, scale=-1.0).then_inc(en_ready[l], 1)
                for u in (2, 3):
                    hi_upto(first + u + 2)
                    act.wait_ge(consumed, done(("in", l, "hq", u - 2)))
                    nc.scalar.activation(hqT[:, 2 * (u - 2):2 * (u - 2) + 2, :], bank(u % 4, 2, SEQ), ACT.Copy).then_inc(proj_a[l], 1)
                act.wait_ge(f_ready[l], 1)
                nc.scalar.activation(en, arg, ACT.Ln).then_inc(logf_ready[l], 1)
                act.wait_ge(fg_abs[l], 1)
                nc.scalar.activation(small_fg[1], small_fg[1], ACT.Exp).then_inc(fg_exp[l], 1)
                act.wait_ge(fg_exp[l], 1)
                nc.scalar.activation(small_fg[1], small_fg[1], ACT.Ln, bias=1.0).then_inc(fg_ln[l], 1)

                dest = [(qT, "fq", 0), (qT, "fq", 1), (kT, "fk", 0), (kT, "fk", 1), (fv, "fv", 0), (fv, "fv", 1),
                        (hv, "hi", 0), (hv, "hi", 1), (hgate, "hg", 0), (hgate, "hg", 1)]
                for j, (to, name, c) in enumerate(dest):
                    u = 5 + j
                    end = done(("in", l, name, c if name in IN_TRANSPOSED else 1))
                    hi_upto(end + 1)
                    act.wait_ge(consumed, end)
                    if to is qT or to is kT:
                        nc.scalar.activation(to[:, 2 * c:2 * c + 2, :], bank(u % 4, 2, SEQ), ACT.Copy,
                                             scale=HD ** -0.5 if to is qT else 1.0).then_inc(proj_a[l], 1)
                    else:
                        nc.scalar.activation(to[:, c, :], bank(u % 4), ACT.Silu if to is hgate else ACT.Copy).then_inc(proj_a[l], 1)
                    if j < len(LEVELS) + 1:
                        act.wait_ge(arg_ready[l], j + 1)
                        nc.scalar.activation(arg, arg, ACT.Exp).then_inc(exp_ready[l], 1)
                hi_upto(first + 16)
                for u, unit in enumerate(UNITS):
                    act.wait_ge(nmax_ready[l], u + 1)
                    if u >= 2:
                        act.wait_ge(pT_psum[l], u - 1)
                    t, par, heads = unit
                    n = NC // len(heads)
                    for i, hd in enumerate(heads):
                        c = t * NH + hd
                        nc.scalar.activation(probs[u % 2][:, i * n:(i + 1) * n], bank(SBANK[u])[:, i * n:(i + 1) * n], ACT.Exp,
                                             bias=nmax[:, c:c + 1], accum_out=rsum[:, c:c + 1]).then_inc(probs_ready[l], 1)
                    if u == 0:
                        for tt in range(TT):
                            act.wait_ge(hgrn_o[l], tt + 1)
                            nc.scalar.activation(un[:, tt, W:2 * W], bank(2 + tt), ACT.Copy).then_inc(hgrn_c[l], 1)
                    if u == 2:
                        act.wait_ge(hgrn_c[l], TT)
                        nc.scalar.activation(sq, un[:, :, W:2 * W], ACT.Square).then_inc(hsq[l], 1)
                    if u == 4:
                        root(hm, hy, hry[l], (hms[l], 1))
                    if u >= 1:
                        pT_out(l, u - 1)
                pT_out(l, len(UNITS) - 1)
                act.wait_ge(fox_n[l], TT)
                nc.scalar.activation(sq, un[:, :, 0:W], ACT.Square).then_inc(hsq[l], 1)
                root(hm, hy, hry[l], (hms[l], 2))
                hi_parts(TURN_MIX[l])

            def pT_out(l, u):
                act.wait_ge(pT_psum[l], u + 1)
                if u >= 2:
                    act.wait_ge(fox_o[l], u - 1)
                nc.scalar.activation(probsT[u % 2], bank(SBANK[u], 4, P), ACT.Copy).then_inc(pT_ready[l], 1)

            def ple(l, ready, gate_in, c):
                hi_upto(c + 2)
                act.wait_ge(pT_ps[l], 1)
                nc.scalar.activation(pT[0], bank(0, PKT, SEQ), ACT.Copy).then_inc(pT_hi[l], 1)
                norm(3 * l + 2, ready, c + 1)
                for jj, j in enumerate(GORDER):
                    t, n = j // 2, j % 2
                    gate_in(n)
                    nc.scalar.activation(sig[:, t, n * NC:(n + 1) * NC], bank(4 + j), ACT.Sigmoid).then_inc(ple_sig[l], 1)

            def turn_hi(i, r):
                act.wait_ge(exT_ps, i * EXR + (r + 1))
                nc.scalar.activation(exhT[0], bank(4, 4, P), ACT.Copy).then_inc(exT_hi, 1)

            act.wait_ge(lb_max, 1)
            nc.scalar.activation(lbb, lba, ACT.Exp).then_inc(lb_exp, 1)

            norm(0, lambda t: act.wait_ge(x_in, 16), -1)
            mixer(0)
            norm(1, lambda t: act.wait_ge(h_ready[1], 2 * TT), STATIC.index(("out", 0, 1, 1)))
            load_wfg(1)
            load_p(0)
            def silu(r):
                n = ff_halves(r) * NC // 2
                end = done(("fg", 0, r, ff_halves(r) - 1))
                hi_upto(end + 1)
                for t in range(TT):
                    act.wait_ge(consumed, end)
                    if r >= 1:
                        act.wait_ge(ffh_ready, 2 * (r - 1) + t + 1)
                    nc.scalar.activation(ffs[t][:, 0:n], bank(t)[:, 0:n], ACT.Silu).then_inc(ffsil, 1)

            def hidden_hi(r):
                nt = 2 * ff_halves(r)
                hi_upto(done(("fg", 0, r + 1, 0) if r + 1 < FFR else ("fu", 0, r, ff_halves(r) - 1)) + 1)
                for t in range(TT):
                    act.wait_ge(ffT_ps, 2 * r + t + 1)
                    nc.scalar.activation(ffT[0][:, t, 0:nt, :], bank(2 + t, 4, P)[:, 0:nt, :], ACT.Copy).then_inc(ffT_hi, 1)

            silu(0)
            for r in range(1, FFR):
                if ff_halves(r) == 2:
                    hidden_hi(r - 1)
                    silu(r)
                else:
                    silu(r)
                    hidden_hi(r - 1)
            hidden_hi(FFR - 1)

            def gate_in(n):
                end = done(("pg", 0, n, 1))
                hi_upto(end + 1)
                act.wait_ge(consumed, end)

            ple(0, lambda t: act.wait_ge(h_ready[2], 2 * TT), gate_in, STATIC.index(("pe", 0, 0, 0)) - 1)
            norm(3, lambda t: act.wait_ge(h_ready[3], 2 * TT), STATIC.index(("pg", 0, 1, 1)))
            mixer(1)
            norm(4, lambda t: act.wait_ge(h_ready[4], 2 * TT), NSTATIC - 1)
            load_p(1)
            act.wait_ge(rdiff, 1)
            nc.scalar.activation(gexp, gdiff, ACT.Exp).then_inc(rexp, 1)

            act.wait_ge(table_ready, 1)
            n_items = act.value_load(item_expert[0:1, ITEMS:ITEMS + 1], min_val=NE, max_val=ITEMS)

            def hi(n, i):
                s = NSTATIC + n
                act.wait_ge(*exp_filled(n, i))
                act.wait_ge(consumed, i * EXP_LOADS + (s - SPLIT + 1))
                nc.scalar.activation(whi[:, s % SPLIT, :], raw[:, s % RAW, :], ACT.Copy).then_inc(hi_a, 1)

            def tokens_hi(i, q):
                act.wait_ge(etmp_ready, i * 2 + (q + 1))
                nc.scalar.activation(uTeh[:, 4 * q:4 * q + 4, :], uTe[:, 4 * q:4 * q + 4, :], ACT.Copy).then_inc(euh_ready, 1)

            for n in range(SPLIT):
                hi(n, 0)
            for q in range(2):
                tokens_hi(0, q)
            with act.Fori(0, n_items) as i:
                for n, (kind, r, hf) in enumerate(EXP_ORDER):
                    if kind == "g" and hf == 0 and r >= 1:
                        turn_hi(i, r - 1)
                    if kind == "g" and hf == 1:
                        act.wait_ge(consumed, i * EXP_LOADS + (NSTATIC + n + 1))
                        nc.scalar.activation(exs[r % 2], bank(r % 2), ACT.Silu).then_inc(exsil, 1)
                    if n == COMB_AT:
                        act.wait_ge(comb_ps, i + 1)
                        nc.scalar.activation(combT, bank(7)[:, 0:SEQ].rearrange("p (a b) -> p a b", a=TT), ACT.Copy).then_inc(comb_ready, 1)
                    if n == LAST_UP:
                        tokens_hi(i + 1, 0)
                        turn_hi(i, r)
                    if n == EXP_LOADS - 1:
                        act.wait_ge(y_half, i + 1)
                        nc.scalar.activation(ye[:, 0:NC], bank(5), ACT.Copy).then_inc(y_a, 1)
                    hi(n + SPLIT, i)
                    if n == LAST_UP:
                        tokens_hi(i + 1, 1)
            act.wait_ge(hacc, n_items * 4 + 1)
            act.dma_start(fgain, final_norm_gain.rearrange("(a d) -> a d", a=1).to_broadcast([P, D])).then_inc(fgain_in, 16)

            tail_hi = [SPLIT]
            def gate_in(n):
                for k in range(tail_hi[0], len(TAIL)):
                    hi(k, n_items)
                    tail_hi[0] = k + 1
                act.wait_ge(consumed, n_items * EXP_LOADS + (NSTATIC + 3 + 2 * n))

            ple(1, lambda t: None, gate_in, NSTATIC)
            norm(6, lambda t: act.wait_ge(h_ready[6], 2 * TT), NSTATIC)

        @block.vector
        def _(dve):
            V = nc.vector
            chain = [0]

            def link(ins):
                chain[0] += 1
                ins.then_inc(dchain, 1)
                dve.wait_ge(dchain, chain[0])

            def refine(v, y, t):
                link(V.reciprocal(y, y))
                link(V.tensor_tensor(t, y, y, ALU.mult))
                link(V.tensor_tensor(t, t, v, ALU.mult))
                link(V.tensor_scalar(t, t, -0.5, 1.5, ALU.mult, ALU.add))
                link(V.tensor_tensor(y, y, t, ALU.mult))

            def norm_stats(k):
                dve.wait_ge(sq_done, k * TT + TT)
                V.tensor_scalar(ms, ssq, 1.0 / D, EPS, ALU.mult, ALU.add).then_inc(ms_ready, 1)
                dve.wait_ge(ms_ready, k + 1)
                dve.wait_ge(ry_ready, k + 1)
                refine(ms, ry, rt)

            def norm(k):
                norm_stats(k)
                for t in range(TT):
                    V.tensor_scalar(un[:, t, :], h[:, t, :], ry[:, t:t + 1], None, ALU.mult).then_inc(un_ready, 1)
                gains(TURN_NORM[k], ROW_NORM(k))

            def gains(turn, row):
                for j in range(2 * TT):
                    t, q = j // 2, j % 2
                    dve.wait_ge(uT_psum, 4 * turn + j + 1)
                    g = vec[:, row + 4 * q:row + 4 * q + 4].unsqueeze(2).to_broadcast([P, 4, P])
                    V.tensor_tensor(uT[:, 4 * q:4 * q + 4, t * P:(t + 1) * P], bank(4 + j, 4, P), g,
                                    ALU.mult).then_inc(tmp_ready, 1)
                for j in range(2 * TT):
                    s = (slice(None), slice(4 * (j % 2), 4 * (j % 2) + 4), slice(j // 2 * P, (j // 2 + 1) * P))
                    dve.wait_ge(uh_ready, 4 * turn + j + 1)
                    V.tensor_tensor(uTl[s], uT[s], uTh[s].bitcast(F32), ALU.subtract).then_inc(uT_ready, 1)

            def add_out(l, ready):
                for j, (t, n) in enumerate([(0, 0), (1, 0), (0, 1), (1, 1)]):
                    dve.wait_ge(consumed, done(("out", l, n, 1)))
                    hv_ = h[:, t, n * NC:(n + 1) * NC]
                    V.tensor_tensor(hv_, bank(j), hv_, ALU.add).then_inc(ready, 1)

            def halves(v, m):
                f = v.rearrange("p a b -> p (a b)").rearrange("p (b u m) -> p b u m", u=2, m=m)
                return f[:, :, 1, :], f[:, :, 0, :]

            def mixer(l):
                for u in range(2):
                    dve.wait_ge(consumed, done(("in", l, "hf", u)))
                    V.tensor_scalar(en[:, 2 * u:2 * u + 2, :], bank(u, 2, SEQ), GATE_FLOOR, None, ALU.max).then_inc(proj_d[l], 1)
                dve.wait_ge(en_ready[l], 1)
                link(V.tensor_scalar(arg, en, 1.0, None, ALU.add))
                link(V.reciprocal(arg, arg))
                link(V.tensor_tensor(keyT, en, arg, ALU.mult))
                for m in range(NP):
                    V.tensor_scalar(keyT[:, m, :], keyT[:, m, :], oml[:, l, m:m + 1], None, ALU.mult).then_inc(dchain, 1)
                    V.tensor_scalar(arg[:, m, :], arg[:, m, :], oml[:, l, m:m + 1], lb[:, l, m:m + 1], ALU.mult,
                                    ALU.add).then_inc(f_ready[l] if m == NP - 1 else dchain, 1)
                    chain[0] += 1 if m == NP - 1 else 2
                dve.wait_ge(fgp[l], 1)
                link(V.tensor_scalar(small_fg[0], bank(0)[:, 0:SEQ], bias[:, l:l + 1], None, ALU.add))
                V.tensor_scalar(small_fg[1], small_fg[0], -1.0, None, ALU.mult).then_inc(dchain, 1)
                chain[0] += 1
                dve.wait_ge(dchain, chain[0])
                V.tensor_tensor(small_fg[1], small_fg[1], small_fg[0], ALU.min).then_inc(fg_abs[l], 1)
                dve.wait_ge(logf_ready[l], 1)
                for m in range(NP):
                    V.tensor_tensor_scan(bT[:, m, :], ones[:, :], en[:, m, :], 0.0, ALU.mult, ALU.add).then_inc(dchain, 1)
                    chain[0] += 1
                dve.wait_ge(fg_ln[l], 1)
                dve.wait_ge(dchain, chain[0])
                link(V.scalar_tensor_tensor(small_fg[0], small_fg[0], 0.0, small_fg[1], ALU.min, ALU.subtract))
                link(V.tensor_tensor_scan(small_fg[1], ones[:, :], small_fg[0], 0.0, ALU.mult, ALU.add))
                V.tensor_scalar(negc[:, :], small_fg[1], -1.0, None, ALU.mult).then_inc(negc_ready[l], 1)

                def args(i):
                    if i >= 1:
                        dve.wait_ge(xl_ready[l], 2 * i)
                    if i < len(LEVELS):
                        m = LEVELS[i]
                        bu, bl = halves(bT, m)
                        au, al = halves(arg, m)
                    else:
                        m = P
                        bu, bl = bT[:, :, P:SEQ], bT[:, :, 0:P]
                        au, al = arg[:, :, P:SEQ], arg[:, :, 0:P]
                    ref = bl[:, :, m - 1:m].to_broadcast(list(bl.shape))
                    V.tensor_tensor(au, bu, ref, ALU.subtract).then_inc(dchain, 1)
                    chain[0] += 1
                    V.tensor_tensor(al, ref, bl, ALU.subtract).then_inc(arg_ready[l], 1)

                def decayed(i):
                    dve.wait_ge(exp_ready[l], i + 1)
                    if i >= 2:
                        dve.wait_ge(lev[l], 4 * i)
                    if i < len(LEVELS):
                        m = LEVELS[i]
                        (qu, _), (_, kl), (au, al), (xu, xlo) = (halves(v, m) for v in (hqT, keyT, arg, xl[i % 2]))
                    else:
                        qu, kl = hqT[:, :, P:SEQ], keyT[:, :, 0:P]
                        au, al, xu, xlo = arg[:, :, P:SEQ], arg[:, :, 0:P], xl[i % 2][:, :, P:SEQ], xl[i % 2][:, :, 0:P]
                    V.tensor_tensor(xu, qu, au, ALU.mult).then_inc(xl_ready[l], 1)
                    V.tensor_tensor(xlo, kl, al, ALU.mult).then_inc(xl_ready[l], 1)

                def take(i):
                    for j in range(4):
                        t, par = j // 2, j % 2
                        dve.wait_ge(lev[l], 4 * i + j + 1)
                        mi = (i - 1) % NL
                        mask = masks[:, mi, :].bitcast(U32).unsqueeze(1).to_broadcast([P, NP, P])
                        V.copy_predicated(scores[:, t, par::2, :], mask, bank(4 + j, NP, P)).then_inc(lev_d[l], 1)

                args(0)
                dve.wait_ge(proj_a[l], 2)
                for i in range(len(LEVELS) + 1):
                    decayed(i)
                    if i < len(LEVELS):
                        args(i + 1)
                    take(i)
                for par in range(2):
                    dve.wait_ge(lev[l], 4 * NL + par + 1)
                    V.tensor_copy(cross[:, par::2, :], bank(4 + par, NP, P)).then_inc(lev_d[l], 1)

                for u, (t, par, heads) in enumerate(UNITS):
                    dve.wait_ge(logits[l], u + 1)
                    n = NC // len(heads)
                    s3 = bank(SBANK[u], len(heads), n)
                    cm = causal[:, :].unsqueeze(1).to_broadcast([P, len(heads), P])
                    link(V.tensor_tensor(s3[:, :, n - P:n], s3[:, :, n - P:n], cm, ALU.add))
                    c0 = t * NH + heads[0]
                    V.tensor_reduce(nmax[:, c0:c0 + 2 * len(heads) - 1:2], s3, AX, ALU.max, negate=True).then_inc(nmax_ready[l], 1)

                def head_norm(half):
                    c0 = W if half == 0 else 0
                    v = un[:, :, c0:c0 + W]
                    if half == 1:
                        dve.wait_ge(probs_ready[l], 2 * NH)
                        link(V.reciprocal(rinv, rsum))
                        for t in range(TT):
                            dve.wait_ge(fox_o[l], 2 if t == 0 else len(UNITS))
                            r = rinv[:, t * NH:(t + 1) * NH].unsqueeze(2).to_broadcast([P, NH, HD])
                            V.tensor_tensor(un[:, t, 0:W].rearrange("p (h d) -> p h d", h=NH), bank(2 + t, NH, HD), r,
                                            ALU.mult).then_inc(fox_n[l], 1)
                    dve.wait_ge(hsq[l], half + 1)
                    link(V.tensor_reduce(hm, sq.rearrange("p t (h d) -> p (t h) d", d=HD), AX, ALU.add))
                    V.tensor_scalar(hm, hm, 1.0 / HD, EPS, ALU.mult, ALU.add).then_inc(hms[l], 1)
                    dve.wait_ge(hms[l], half + 1)
                    dve.wait_ge(hry[l], half + 1)
                    refine(hm, hy, ht)
                    for t in range(TT):
                        vt = v[:, t, :].rearrange("p (h d) -> p h d", h=NH)
                        y = hy[:, t * NH:(t + 1) * NH].unsqueeze(2).to_broadcast([P, NH, HD])
                        if half == 0:
                            link(V.tensor_tensor(vt, vt, y, ALU.mult))
                            V.tensor_tensor(v[:, t, :], v[:, t, :], hgate[:, t, :], ALU.mult).then_inc(mix_ready[l], 1)
                        else:
                            if t == 0:
                                dve.wait_ge(fox_n[l], TT)
                            V.tensor_tensor(vt, vt, y, ALU.mult).then_inc(mix_ready[l], 1)

                dve.wait_ge(proj_a[l], 12)
                head_norm(0)
                head_norm(1)
                gains(TURN_MIX[l], ROW_OUT + l * KT)
                add_out(l, h_ready[3 * l + 1])

            def ple(l, after_norm=lambda: None):
                dve.wait_ge(pT_hi[l], 1)
                V.tensor_tensor(pT[1], bank(0, PKT, SEQ), pT[0].bitcast(F32), ALU.subtract).then_inc(pT_rd[l], 1)
                norm(3 * l + 2)
                after_norm()
                for jj, j in enumerate(GORDER):
                    t, n = j // 2, j % 2
                    dve.wait_ge(ple_sig[l], jj + 1)
                    s = slice(n * NC, (n + 1) * NC)
                    link(V.tensor_tensor(prod[:, t, s], bank(j), sig[:, t, s], ALU.mult))
                    V.tensor_tensor(h[:, t, s], h[:, t, s], prod[:, t, s], ALU.add).then_inc(h_ready[3 * l + 3], 1)

            dve.wait_ge(vec_T, 1)
            V.tensor_copy(vec[:, :], bank(0)[:, 0:P]).then_inc(vec_ready, 1)
            dve.wait_ge(vec_ready, 1)
            l0, l1 = (vec[:, ROW_LB + l * NP:ROW_LB + (l + 1) * NP] for l in range(2))
            link(V.tensor_tensor(lbc, l0, l1, ALU.max))
            V.tensor_tensor(lba[:, 0:NP], l0, lbc, ALU.subtract).then_inc(dchain, 1)
            chain[0] += 1
            V.tensor_tensor(lba[:, NP:2 * NP], l1, lbc, ALU.subtract).then_inc(lb_max, 1)
            dve.wait_ge(lb_exp, 1)
            link(V.tensor_tensor(lbc, lbb[:, 0:NP], lbb[:, NP:2 * NP], ALU.add))
            link(V.reciprocal(lbc, lbc))
            link(V.memset(lb[:, 0, :], 0.0))
            link(V.tensor_tensor(lb[:, 1, :], lbb[:, NP:2 * NP], lbc, ALU.mult))
            link(V.tensor_scalar(oml[:, :, :], lb[:, :, :], -1.0, 1.0, ALU.mult, ALU.add))
            dve.wait_ge(small_in, 48)

            norm(0)
            mixer(0)
            norm(1)
            def hidden(r):
                n = ff_halves(r) * NC // 2
                for t in range(TT):
                    dve.wait_ge(ffsil, 2 * r + t + 1)
                    dve.wait_ge(consumed, done(("fu", 0, r, ff_halves(r) - 1)))
                    V.tensor_tensor(ffh[t][:, 0:n], bank(2 + t)[:, 0:n], ffs[t][:, 0:n], ALU.mult).then_inc(ffh_ready, 1)

            def hidden_lo(r):
                nt = 2 * ff_halves(r)
                for t in range(TT):
                    dve.wait_ge(ffT_hi, 2 * r + t + 1)
                    V.tensor_tensor(ffT[1][:, t, 0:nt, :], bank(2 + t, 4, P)[:, 0:nt, :], ffT[0][:, t, 0:nt, :].bitcast(F32),
                                    ALU.subtract).then_inc(ffT_ready, 1)

            for r in range(FFR):
                hidden(r)
                hidden_lo(r)
            for j in range(4):
                t, n = j // 2, j % 2
                dve.wait_ge(consumed, done(("fd", 0, FFR - 1, ff_halves(FFR - 1) - 1)))
                hv_ = h[:, t, n * NC:(n + 1) * NC]
                V.tensor_tensor(hv_, bank(4 + j), hv_, ALU.add).then_inc(h_ready[2], 1)
            ple(0)
            norm(3)
            mixer(1)
            norm(4)

            dve.wait_ge(rlog, 1)
            link(V.tensor_copy(logit, bank(0)[:, 0:2 * NE]))
            for t in range(TT):
                c = slice(t * NE, (t + 1) * NE)
                link(V.max(top[:, c], logit[:, c]))
                link(V.max_index(topi[:, c], top[:, c], logit[:, c]))
            link(V.tensor_copy(topf, topi))
            t2 = top.rearrange("p (t e) -> p t e", t=TT)
            V.tensor_tensor(gdiff, t2[:, :, 1], t2[:, :, 0], ALU.subtract).then_inc(rdiff, 1)
            for t in range(TT):
                c = slice(t * NE, (t + 1) * NE)
                link(V.tensor_scalar(oh1[:, c], iota[:, 0:NE], topf[:, t * NE:t * NE + 1], None, ALU.is_equal))
                link(V.tensor_scalar(oh2[:, c], iota[:, 0:NE], topf[:, t * NE + 1:t * NE + 2], None, ALU.is_equal))
            V.tensor_tensor(selected, oh1, oh2, ALU.add).then_inc(sel_count, 1)
            dve.wait_ge(rexp, 1)
            link(V.tensor_scalar(g1, gexp, 1.0, None, ALU.add))
            link(V.reciprocal(g1, g1))
            link(V.tensor_tensor(g2, gexp, g1, ALU.mult))
            for t in range(TT):
                c = slice(t * NE, (t + 1) * NE)
                link(V.tensor_scalar(oh1[:, c], oh1[:, c], g1[:, t:t + 1], None, ALU.mult))
                link(V.scalar_tensor_tensor(table[:, 2 + t, :], oh2[:, c], g2[:, t:t + 1], oh1[:, c], ALU.mult, ALU.add))
            link(V.tensor_copy(table[:, 4, :], iota[:, 0:NE]))
            dve.wait_ge(ranks, 1)
            dve.wait_ge(sel_count, 1)
            for t in range(TT):
                c = slice(t * NE, (t + 1) * NE)
                link(V.scalar_tensor_tensor(table[:, t, :], bank(1)[:, c], 1.0, selected[:, c], ALU.add, ALU.mult))
                link(V.tensor_scalar(table[:, t, :], table[:, t, :], -1.0, None, ALU.add))
            link(V.tensor_scalar(over, bank(1)[:, 2 * NE:3 * NE], float(P), None, ALU.is_gt))
            link(V.tensor_tensor_scan(nover, ones[:, 0:NE], over, 0.0, ALU.mult, ALU.add))
            link(V.memset(items, -1.0))
            link(V.tensor_copy(items[:, :, 0:NE], table))
            for n in range(OVER):
                link(V.tensor_scalar(hot, nover, float(n + 1), None, ALU.is_equal))
                link(V.tensor_tensor(hot, hot, over, ALU.mult))
                link(V.tensor_tensor(tprod, table, hot.unsqueeze(1).to_broadcast([P, 5, NE]), ALU.mult))
                link(V.tensor_reduce(items[:, :, NE + n], tprod, AX, ALU.add))
            link(V.tensor_scalar(items[:, 0:2, NE:ITEMS], items[:, 0:2, NE:ITEMS], -float(P), None, ALU.add))
            V.tensor_scalar(items[:, 4, ITEMS:ITEMS + 1], nover[:, NE - 1:NE], float(NE), None, ALU.add).then_inc(hacc, 1)
            dve.wait_ge(hacc, 1)
            V.tensor_copy(item_expert[:, :], items[:, 4, :]).then_inc(table_ready, 1)
            dve.wait_ge(table_ready, 1)

            n_items = dve.value_load(item_expert[0:1, ITEMS:ITEMS + 1], min_val=NE, max_val=ITEMS)

            def select(i):
                V.tensor_scalar(iitem.unsqueeze(2), items[:, 0:4, bass.ds(i, 1)], 1.0, None, ALU.mult).then_inc(mchain, 1)
                dve.wait_ge(mchain, i * 3 + 1)
                for t in range(TT):
                    V.tensor_scalar(sel[:, t, :], iota[:, :], iitem[:, t:t + 1], None, ALU.is_equal).then_inc(mchain, 1)
                    dve.wait_ge(mchain, i * 3 + (t + 2))
                    V.tensor_scalar(selg[:, t, :], sel[:, t, :], iitem[:, 2 + t:3 + t], None, ALU.mult).then_inc(sel_ready, 1)

            def tokens(i, q):
                dve.wait_ge(gath, i * 2 + (q + 1))
                row = ROW_NORM(4) + 4 * q
                g = vec[:, row:row + 4].unsqueeze(2).to_broadcast([P, 4, P])
                V.tensor_tensor(uTe[:, 4 * q:4 * q + 4, :], bank(GATHER_BANKS[q], 4, P), g, ALU.mult).then_inc(etmp_ready, 1)

            def tokens_lo(i):
                for q in range(2):
                    s = slice(4 * q, 4 * q + 4)
                    dve.wait_ge(euh_ready, i * 2 + (q + 1))
                    V.tensor_tensor(uTel[:, s, :], uTe[:, s, :], uTeh[:, s, :].bitcast(F32), ALU.subtract).then_inc(uTe_ready, 1)

            def lo(n, i):
                dve.wait_ge(hi_a, i * EXP_LOADS + (NSTATIC + n + 1))
                lo_part(nc.vector, NSTATIC + n, 0, LO_DVE).then_inc(lo_d, 1)

            select(0)
            for n in range(SPLIT):
                lo(n, 0)
            for q in range(2):
                tokens(0, q)
            tokens_lo(0)
            with dve.Fori(0, n_items) as i:
                def turn_lo(r):
                    dve.wait_ge(exT_hi, i * EXR + (r + 1))
                    V.tensor_tensor(exhT[1], bank(4, 4, P), exhT[0].bitcast(F32), ALU.subtract).then_inc(exT_ready, 1)

                for n, (kind, r, hf) in enumerate(EXP_ORDER):
                    if kind == "g" and hf == 0 and r >= 1:
                        turn_lo(r - 1)
                    if n == SELECT_AT:
                        select(i + 1)
                    if kind == "u" and hf == 1:
                        dve.wait_ge(exsil, i * EXR + (r + 1))
                        dve.wait_ge(consumed, i * EXP_LOADS + (NSTATIC + n + 1))
                        V.tensor_tensor(exh[r % 2], bank(2 + r % 2), exs[r % 2], ALU.mult).then_inc(exh_ready, 1)
                    if n == LAST_UP:
                        tokens(i + 1, 0)
                        turn_lo(r)
                    if n < EXP_LOADS - 1:
                        lo(n + SPLIT, i)
                    if n == LAST_UP:
                        tokens(i + 1, 1)
                        tokens_lo(i + 1)
                dve.wait_ge(consumed, i * EXP_LOADS + (NSTATIC + EXP_LOADS))
                V.tensor_copy(ye[:, NC:D], bank(6)).then_inc(y_d, 1)
                for j, (t, n) in enumerate(COMBINE):
                    dve.wait_ge(comb, i * 4 + (j + 1))
                    hv_ = h[:, t, n * NC:(n + 1) * NC]
                    V.tensor_tensor(hv_, bank(COMBINE_BANKS[j]), hv_, ALU.add).then_inc(hacc, 1)
                lo(EXP_LOADS - 1 + SPLIT, i)
            dve.wait_ge(hacc, n_items * 4 + 1)
            ple(1, lambda: [lo(k, n_items) for k in range(SPLIT, len(TAIL))])
            norm_stats(6)
            dve.wait_ge(fgain_in, 16)
            for t in range(TT):
                link(V.tensor_scalar(fout[:, t, :], h[:, t, :], ry[:, t:t + 1], None, ALU.mult))
                V.tensor_tensor(fout[:, t, :], fout[:, t, :], fgain, ALU.mult).then_inc(out_ready, 1)

        @block.tensor
        def _(pe):
            T = nc.tensor

            def norm(k):
                for t in range(TT):
                    pe.wait_ge(un_ready, k * TT + t + 1)
                    transposes(t)

            def transposes(t):
                for q in range(2):
                    for c in range(4):
                        last = T.transpose(bank(4 + 2 * t + q, 4, P)[:, c, :], un[:, t, (4 * q + c) * P:(4 * q + c + 1) * P], ident[:, :])
                    last.then_inc(uT_psum, 1)

            def product(o, sth, stl, mvh, mvl, start, stop):
                T.matmul(o, sth, mvh, start=start, stop=False)
                T.matmul(o, sth, mvl, start=False, stop=False)
                return T.matmul(o, stl, mvh, start=False, stop=stop)

            def parts(n, k):
                return as_k(whi[:, n % SPLIT, :], k), as_k(wlo[:, n % SPLIT, :], k)

            def arrived(key):
                n = STATIC.index(key)
                pe.wait_ge(lo_s, n + 1)
                return parts(n, source(key).shape[1])

            def both_tiles(banks, w, hf, nk):
                wh, wl = w
                for t in range(TT):
                    s = slice(t * P, (t + 1) * P)
                    for k in range(nk):
                        kk = hf * HALF + k
                        last = product(banks[t], uTh[:, kk, s], uTl[:, kk, s], wh[:, k, :], wl[:, k, :],
                                       start=kk == 0, stop=kk == KT - 1)
                last.then_inc(consumed, 1)

            def mixer(l):
                unit = [0]

                def begin():
                    u = unit[0]
                    if u == 4:
                        pe.wait_ge(proj_d[l], 1)
                    elif u in (5,):
                        pe.wait_ge(proj_d[l], 2)
                    elif u in (6, 7):
                        pe.wait_ge(proj_a[l], u - 5)
                    elif u == 8:
                        pe.wait_ge(fg_abs[l], 1)
                    elif u >= 9:
                        pe.wait_ge(proj_a[l], u - 6)
                    unit[0] += 1
                    return u % 4

                def transposed(name, c):
                    o = bank(begin(), 2, SEQ)
                    wh, wl = arrived(("in", l, name, c))
                    for m in range(2):
                        s = slice(m * P, (m + 1) * P)
                        for k in range(KT):
                            last = product(o[:, m, :], wh[:, k, s], wl[:, k, s], uTh[:, k, :], uTl[:, k, :],
                                           start=k == 0, stop=k == KT - 1)
                    last.then_inc(consumed, 1)

                def level(i):
                    if i == 0:
                        pe.wait_ge(logf_ready[l], 1)
                        pe.wait_ge(proj_a[l], 2)
                    else:
                        pe.wait_ge(xl_ready[l], 2 * i)
                    if i >= 1:
                        pe.wait_ge(lev_d[l], 4 * i)
                    left, right = (keyT, hqT) if i == 0 else (xl[(i - 1) % 2], xl[(i - 1) % 2])
                    for t in range(TT if i < NL else 1):
                        for par in range(2):
                            b = bank(4 + 2 * t + par, NP, P)
                            r = slice(par * HD, (par + 1) * HD)
                            ts_, tt_ = (t, t) if i < NL else (0, 1)
                            for m in range(NP):
                                last = T.matmul(b[:, m, :], left[r, m, ts_ * P:(ts_ + 1) * P],
                                                right[r, m, tt_ * P:(tt_ + 1) * P], start=True, stop=True)
                            last.then_inc(lev[l], 1)

                for name in IN_ORDER[0:2]:
                    for c in range(2):
                        transposed(name, c)
                pe.wait_ge(wfg_in[l], 32)
                b = begin()
                for k in range(KT):
                    last = T.matmul(bank(b)[:, 0:SEQ], wfg[:, k, :], uT[:, k, :], start=k == 0, stop=k == KT - 1)
                last.then_inc(fgp[l], 1)
                grp = 0
                for name in IN_ORDER[2:]:
                    if name not in IN_TRANSPOSED:
                        banks = [bank(begin()) for t in range(TT)]
                    for c in range(2):
                        if name in IN_TRANSPOSED:
                            transposed(name, c)
                        else:
                            both_tiles(banks, arrived(("in", l, name, c)), c, HALF)
                        if grp <= NL and (name != "fq" or c == 1):
                            level(grp)
                            grp += 1
                assert grp == NL + 1
                pe.wait_ge(negc_ready[l], 1)
                pe.wait_ge(proj_a[l], 6)
                for u, (t, par, heads) in enumerate(UNITS):
                    if u == 0:
                        pe.wait_ge(lev_d[l], 4 * NL + 2)
                    if u == 4:
                        pe.wait_ge(proj_a[l], 12)
                    n = NC // len(heads)
                    r = slice(par * HD, (par + 1) * HD)
                    for i, hd in enumerate(heads):
                        o = bank(SBANK[u])[:, i * n:(i + 1) * n]
                        T.matmul(o, qT[r, hd // 2, t * P:(t + 1) * P], kT[r, hd // 2, 0:n], start=True, stop=False)
                        last = T.matmul(o, pick[r, hd, :], negc[r, 0:n], start=False, stop=True)
                    last.then_inc(logits[l], 1)
                for t in range(TT):
                    for hd in range(NH):
                        o = bank(2 + t)[:, hd * HD:(hd + 1) * HD]
                        if t == 1:
                            T.matmul(o, cross[:, hd, :], hv[:, 0, hd * HD:(hd + 1) * HD], start=True, stop=False)
                        last = T.matmul(o, scores[:, t, hd, :], hv[:, t, hd * HD:(hd + 1) * HD], start=t == 0, stop=True)
                    last.then_inc(hgrn_o[l], 1)

                def attend(u):
                    t, par, heads = UNITS[u]
                    pe.wait_ge(pT_ready[l], u + 1)
                    if u == 0:
                        pe.wait_ge(hgrn_c[l], TT)
                    nk = t + 1
                    for i, hd in enumerate(heads):
                        for kt in range(nk):
                            last = T.matmul(bank(2 + t)[:, hd * HD:(hd + 1) * HD], probsT[u % 2][:, i * nk + kt, :],
                                            fv[:, kt, hd * HD:(hd + 1) * HD], start=kt == 0, stop=kt == nk - 1)
                    last.then_inc(fox_o[l], 1)

                ph = 0
                for u, (t, par, heads) in enumerate(UNITS):
                    ph += len(heads)
                    pe.wait_ge(probs_ready[l], ph)
                    for c in range(4):
                        last = T.transpose(bank(SBANK[u], 4, P)[:, c, :], probs[u % 2][:, c * P:(c + 1) * P], ident[:, :])
                    last.then_inc(pT_psum[l], 1)
                    if u >= 1:
                        attend(u - 1)
                attend(len(UNITS) - 1)
                pe.wait_ge(mix_ready[l], 2 * TT)
                for t in range(TT):
                    transposes(t)
                pe.wait_ge(uT_ready, 4 * TURN_MIX[l] + 4)
                for n in range(2):
                    for hf in range(2):
                        both_tiles([bank(2 * n + t) for t in range(TT)], arrived(("out", l, n, hf)), hf, HALF)

            def ple(l, chunk_in):
                pe.wait_ge(p_in[l], 16)
                for t in range(TT):
                    for k in range(PKT):
                        last = T.transpose(bank(0, PKT, SEQ)[:, k, t * P:(t + 1) * P], pn[:, t, k * P:(k + 1) * P], ident[:, :])
                last.then_inc(pT_ps[l], 1)
                wh, wl = chunk_in(0)
                pe.wait_ge(pT_rd[l], 1)
                for j in range(4):
                    s, c = slice(j // 2 * P, (j // 2 + 1) * P), slice(j % 2 * NC, (j % 2 + 1) * NC)
                    for k in range(PKT):
                        last = product(bank(j), pT[0][:, k, s], pT[1][:, k, s], wh[:, k, c], wl[:, k, c],
                                       start=k == 0, stop=k == PKT - 1)
                last.then_inc(consumed, 1)
                norm(3 * l + 2)
                pe.wait_ge(uT_ready, 4 * TURN_NORM[3 * l + 2] + 4)
                for n in range(2):
                    for hf in range(2):
                        both_tiles([bank(4 + 2 * t + n) for t in range(TT)], chunk_in(1 + 2 * n + hf), hf, HALF)

            pe.wait_ge(consts, CONSTS)
            pe.wait_ge(vec_in, 16 * (3 + 3 * DEPTH))
            T.transpose(bank(0)[:, 0:P], rows[:, :], ident[:, :]).then_inc(vec_T, 1)

            norm(0)
            pe.wait_ge(uT_ready, 4 * TURN_NORM[0] + 4)
            mixer(0)
            norm(1)
            pe.wait_ge(uT_ready, 4 * TURN_NORM[1] + 4)

            def gate_up(kind, r, hf):
                nh = ff_halves(r)
                b0 = 0 if kind == "fg" else 2
                both_tiles([bank(b0 + t)[:, 0:nh * NC // 2] for t in range(TT)], arrived((kind, 0, r, hf)),
                           hf, HALF if nh == 2 else KT)

            def turn_hidden(r):
                for t in range(TT):
                    pe.wait_ge(ffh_ready, 2 * r + t + 1)
                    for c in range(2 * ff_halves(r)):
                        last = T.transpose(bank(2 + t, 4, P)[:, c, :], ffh[t][:, c * P:(c + 1) * P], ident[:, :])
                    last.then_inc(ffT_ps, 1)

            def down(r):
                pe.wait_ge(ffT_ready, 2 * r + 2)
                for hf in range(ff_halves(r)):
                    wh, wl = arrived(("fd", 0, r, hf))
                    for c in range(2):
                        cc = 2 * hf + c
                        end = r == FFR - 1 and cc == 2 * ff_halves(r) - 1
                        for j in range(4):
                            t, s = j // 2, slice(j % 2 * NC, (j % 2 + 1) * NC)
                            last = product(bank(4 + j), ffT[0][:, t, cc, :], ffT[1][:, t, cc, :], wh[:, c, s], wl[:, c, s],
                                           start=r == 0 and cc == 0, stop=end)
                    last.then_inc(consumed, 1)

            for r in range(FFR):
                if r >= 1:
                    pe.wait_ge(ffsil, 2 * r)
                gate_up("fg", r, 0)
                if r >= 1:
                    turn_hidden(r - 1)
                if ff_halves(r) == 2:
                    gate_up("fg", r, 1)
                if r >= 1:
                    down(r - 1)
                for hf in range(ff_halves(r)):
                    gate_up("fu", r, hf)
            turn_hidden(FFR - 1)
            down(FFR - 1)
            PLE0 = ple_chunks(0)
            ple(0, lambda k: arrived(PLE0[k]))
            norm(3)
            pe.wait_ge(uT_ready, 4 * TURN_NORM[3] + 4)
            mixer(1)
            norm(4)
            pe.wait_ge(uT_ready, 4 * TURN_NORM[4] + 4)
            pe.wait_ge(small_in, 48)
            for t in range(TT):
                for k in range(KT):
                    last = T.matmul(bank(0)[:, t * NE:(t + 1) * NE], uT[:, k, t * P:(t + 1) * P], wr[:, k, :], start=k == 0, stop=k == KT - 1)
            last.then_inc(rlog, 1)
            pe.wait_ge(sel_count, 1)
            s0, s1 = selected[:, 0:NE], selected[:, NE:2 * NE]
            one = ones[:, 0:P]
            T.matmul(bank(1)[:, 0:NE], before[:, :], s0, start=True, stop=True)
            T.matmul(bank(1)[:, NE:2 * NE], one, s0, start=True, stop=False)
            T.matmul(bank(1)[:, NE:2 * NE], before[:, :], s1, start=False, stop=True)
            T.matmul(bank(1)[:, 2 * NE:3 * NE], one, s0, start=True, stop=False)
            T.matmul(bank(1)[:, 2 * NE:3 * NE], one, s1, start=False, stop=True).then_inc(ranks, 1)

            pe.wait_ge(table_ready, 1)
            n_items = pe.value_load(item_expert[0:1, ITEMS:ITEMS + 1], min_val=NE, max_val=ITEMS)

            def gather(i, q):
                pe.wait_ge(sel_ready, i * 2 + 2)
                for c in range(4):
                    for t in range(TT):
                        k = 4 * q + c
                        last = T.matmul(bank(GATHER_BANKS[q], 4, P)[:, c, :], un[:, t, k * P:(k + 1) * P], sel[:, t, :],
                                        start=t == 0, stop=t == 1)
                last.then_inc(gath, 1)

            for q in range(2):
                gather(0, q)
            with pe.Fori(0, n_items) as i:
                def chunk_in(n, k):
                    pe.wait_ge(lo_d, i * EXP_LOADS + (n + 1))
                    pe.wait_ge(lo_p, i * EXP_LOADS + (n + 1))
                    return parts(NSTATIC + n, k)

                def turn(r):
                    pe.wait_ge(exh_ready, i * EXR + (r + 1))
                    for c in range(4):
                        last = T.transpose(bank(4, 4, P)[:, c, :], exh[r % 2][:, c * P:(c + 1) * P], ident[:, :])
                    last.then_inc(exT_ps, 1)

                pe.wait_ge(uTe_ready, i * 2 + 2)
                for n, (kind, r, hf) in enumerate(EXP_ORDER):
                    if kind == "d":
                        if hf == 0:
                            pe.wait_ge(exT_ready, i * EXR + (r + 1))
                        wh, wl = chunk_in(n, 2)
                        end = n == EXP_LOADS - 1
                        for c, q in ([(c, q) for q in range(2) for c in range(2)] if end else
                                     [(c, q) for c in range(2) for q in range(2)]):
                            cc = 2 * hf + c
                            s = slice(q * NC, (q + 1) * NC)
                            last = product(bank(5 + q), exhT[0][:, cc, :], exhT[1][:, cc, :], wh[:, c, s], wl[:, c, s],
                                           start=r == 0 and cc == 0, stop=end and c == 1)
                            if end and (c, q) == (1, 0):
                                last.then_inc(y_half, 1)
                    else:
                        if hf == 0 and r >= 2:
                            pe.wait_ge(exh_ready, i * EXR + (r - 1))
                        if (kind, r, hf) == ("u", 0, 0):
                            pe.wait_ge(hacc, i * 4 + 1)
                        wh, wl = chunk_in(n, HALF)
                        for k in range(HALF):
                            kk = hf * HALF + k
                            last = product(bank((0 if kind == "g" else 2) + r % 2), uTeh[:, kk, :], uTel[:, kk, :],
                                           wh[:, k, :], wl[:, k, :], start=kk == 0, stop=kk == KT - 1)
                    last.then_inc(consumed, 1)
                    if kind == "g" and hf == 0 and r >= 1:
                        turn(r - 1)
                    if n == COMB_AT:
                        for t in range(TT):
                            last = T.transpose(bank(7)[:, t * P:(t + 1) * P], selg[:, t, :], ident[:, :])
                        last.then_inc(comb_ps, 1)
                    if n == LAST_UP:
                        pe.wait_ge(comb_ready, i + 1)
                        gather(i + 1, 0)
                        turn(r)
                        gather(i + 1, 1)
                pe.wait_ge(etmp_ready, i * 2 + 4)
                pe.wait_ge(y_a, i + 1)
                for j, (t, n) in enumerate(COMBINE):
                    if n == 1 and t == 0:
                        pe.wait_ge(y_d, i + 1)
                    T.matmul(bank(COMBINE_BANKS[j]), combT[:, t, :], ye[:, n * NC:(n + 1) * NC], start=True, stop=True).then_inc(comb, 1)

            def tail_in(k):
                pe.wait_ge(lo_d, n_items * EXP_LOADS + (k + 1))
                pe.wait_ge(lo_p, n_items * EXP_LOADS + (k + 1))
                return parts(NSTATIC + k, PKT if k == 0 else HALF)

            pe.wait_ge(hacc, n_items * 4 + 1)
            ple(1, tail_in)


UNITS = [(0, 0, [0, 2, 4, 6]), (0, 1, [1, 3, 5, 7]),
         (1, 0, [0, 2]), (1, 1, [1, 3]), (1, 0, [4, 6]), (1, 1, [5, 7])]
SBANK = [4, 5, 6, 7, 0, 1]
GORDER = [0, 2, 1, 3]
COMB_AT = 4
LAST_UP = EXP_ORDER.index(("u", EXR - 1, 1))
SELECT_AT = LAST_UP - 4
GATHER_BANKS = [1, 7]
COMBINE = [(0, 0), (1, 0), (0, 1), (1, 1)]
COMBINE_BANKS = [3, 1, 7, 2]
ZEROED = 10
CONSTS = 7 + 2 * len(LEVELS)

_INS = ['x', 'p', 'w_in', 'fox_gate_bias', 'fox_out_gain', 'hgrn_lb_logits', 'hgrn_out_gain', 'w_out',
        'mix_norm_gain', 'ffn_norm_gain', 'ple_norm_gain', 'w_ffn_gate', 'w_ffn_up', 'w_ffn_down', 'w_router',
        'w_exp_gate', 'w_exp_up', 'w_exp_down', 'w_ple', 'w_ple_gate', 'final_norm_gain']
_OUTS = [((1, SEQ, D), 'float32')]


def kernel(**inputs):
    import numpy as _np
    import concourse.bacc as _bacc
    from concourse import mybir as _mybir
    from concourse.bass_utils import run_bass_kernel_spmd as _run

    nc = _bacc.Bacc("TRN2", target_bir_lowering=False, num_devices=1, dynamic_dma_scratch_size=2048)
    arrays, args = {}, []
    for name in _INS:
        a = _np.ascontiguousarray(inputs[name])
        arrays[f"in_{name}_dram"] = a
        args.append(nc.dram_tensor(f"in_{name}_dram", a.shape, _mybir.dt.from_np(a.dtype), kind="ExternalInput").ap())
    for i, (shape, dtype) in enumerate(_OUTS):
        dt = _mybir.dt.from_np(_np.dtype(dtype))
        args.append(nc.dram_tensor(f"out_{i}_dram", shape, dt, kind="ExternalOutput").ap())
    trunk(nc, *args)
    r = _run(nc, [arrays], core_ids=[0])
    got = tuple(r.results[0][f"out_{i}_dram"] for i in range(len(_OUTS)))
    return got[0]
```
